# Optimizing a Trainium2 kernel written in Bass

```python
import math
import jax
import jax.numpy as jnp
from jax import lax
import numpy as np

D_MODEL = 1024
BATCH = 1
SEQ = 512
DEPTH = 2
DEC_BATCH = 8
DEC_SEQ = 16
PAST_LEN = 128

CHUNK = 64
Q_BLOCK = 128
N_EVEN = (DEPTH + 1) // 2
N_ODD = DEPTH // 2
D_FF = ((8 * D_MODEL // 3 + 127) // 128) * 128
EPS = 1e-6
NEG_INF = -1e30
LRU_W = D_MODEL // 2
LRU_BLOCKS = 8
LRU_BLOCK = LRU_W // LRU_BLOCKS
LRU_C = 8.0
CONV_W = 4
FOX_HEADS = 8
FOX_DH = (D_MODEL // 2) // FOX_HEADS
FOX_W = FOX_HEADS * FOX_DH
EVEN_MIX_W = LRU_W + FOX_W
EVEN_PROJ = 2 * LRU_W + 3 * FOX_W + FOX_HEADS
DIFF_HEADS = 8
DIFF_DH = D_MODEL // (2 * DIFF_HEADS)
DIFF_W = DIFF_HEADS * 2 * DIFF_DH
ROT_DIM = DIFF_DH // 4
ROPE_THETA = 500000.0

kernel_name = 'streaming_hybrid_rglru_fox_diffattn_step'

def _rmsnorm(x, g):
    xf = x.astype(jnp.float32)
    y = xf * lax.rsqrt(jnp.mean(xf * xf, axis=-1, keepdims=True) + EPS)
    return (y * g.astype(jnp.float32)).astype(x.dtype)

def _swiglu(x, w_in, w_out):
    g, u = jnp.split(x @ w_in, 2, axis=-1)
    return (jax.nn.silu(g) * u) @ w_out

def _rope(x, pos):
    half = ROT_DIM // 2
    inv = ROPE_THETA ** (-jnp.arange(half, dtype=jnp.float32) * (2.0 / ROT_DIM))
    ang = pos.astype(jnp.float32)[:, None] * inv[None, :]
    shape = (ang.shape[0],) + (1,) * (x.ndim - 3) + (half,)
    cos = jnp.cos(ang).reshape(shape).astype(x.dtype)
    sin = jnp.sin(ang).reshape(shape).astype(x.dtype)
    x1 = x[..., :half]
    x2 = x[..., half:ROT_DIM]
    return jnp.concatenate([x1 * cos - x2 * sin, x2 * cos + x1 * sin, x[..., ROT_DIM:]], axis=-1)

def _over_query_blocks(fn, qpos, *qs):
    T = qpos.shape[0]
    if T <= Q_BLOCK:
        return fn(qpos, *qs)
    nb = T // Q_BLOCK

    def split(a):
        return jnp.moveaxis(a.reshape(a.shape[0], nb, Q_BLOCK, *a.shape[2:]), 1, 0)

    out = lax.map(lambda args: fn(args[0], *args[1:]),
                  (qpos.reshape(nb, Q_BLOCK),) + tuple(split(a) for a in qs))
    out = jnp.moveaxis(out, 0, 1)
    return out.reshape(out.shape[0], T, *out.shape[3:])

def _causal_conv(u, buf, w, b):
    T = u.shape[1]
    full = jnp.concatenate([buf.astype(u.dtype), u], axis=1)
    y = b
    for j in range(CONV_W):
        y = y + full[:, j:j + T] * w[j]
    return y, full[:, T:]

def _rglru(u, h0, w_gates, b_gates, lam):
    B, T, C = u.shape
    ub = u.reshape(B, T, LRU_BLOCKS, LRU_BLOCK)
    gates = (jnp.einsum('btnc,ncg->btng', ub, w_gates) + b_gates).astype(jnp.float32)
    r = jax.nn.sigmoid(gates[..., :LRU_BLOCK]).reshape(B, T, C)
    i = jax.nn.sigmoid(gates[..., LRU_BLOCK:]).reshape(B, T, C)
    log_a = -LRU_C * r * jax.nn.softplus(-lam.astype(jnp.float32))
    a = jnp.exp(log_a)
    bx = jnp.sqrt(-jnp.expm1(2.0 * log_a)) * (i * u.astype(jnp.float32))
    bx = bx.at[:, 0].add(a[:, 0] * h0.astype(jnp.float32))

    def combine(left, right):
        a_l, b_l = left
        a_r, b_r = right
        return a_l * a_r, a_r * b_l + b_r

    _, h = lax.associative_scan(combine, (a, bx), axis=1)
    return h, h[:, -1]

def _even_mixer(h, pos, fk_past, fv_past, flogf_past, lru_h0, lru_buf,
                w_in, b_f, conv_w, conv_b, w_gates, b_gates, lam, w_out):
    B, T, _ = h.shape
    cuts = [LRU_W, 2 * LRU_W, 2 * LRU_W + FOX_W, 2 * LRU_W + 2 * FOX_W, 2 * LRU_W + 3 * FOX_W]
    u, gate, q, k, v, f_logit = jnp.split(h @ w_in, cuts, axis=-1)
    uc, new_buf = _causal_conv(u, lru_buf, conv_w, conv_b)
    hs, h_last = _rglru(uc, lru_h0, w_gates, b_gates, lam)
    y_a = hs.astype(h.dtype) * jax.nn.gelu(gate)
    q = q.reshape(B, T, FOX_HEADS, FOX_DH) * (FOX_DH ** -0.5)
    k = k.reshape(B, T, FOX_HEADS, FOX_DH)
    v = v.reshape(B, T, FOX_HEADS, FOX_DH)
    logf = jax.nn.log_sigmoid((f_logit + b_f).astype(jnp.float32))
    P = fk_past.shape[1]
    k_all = jnp.concatenate([fk_past.astype(k.dtype), k], axis=1)
    v_all = jnp.concatenate([fv_past.astype(v.dtype), v], axis=1)
    c_all = jnp.cumsum(jnp.concatenate([flogf_past.astype(jnp.float32), logf], axis=1), axis=1)
    c_keys = c_all.transpose(0, 2, 1)[:, :, None, :]
    c_q = c_all[:, P:]
    kpos = jnp.arange(P + T, dtype=jnp.int32)

    def block(qp, qb, cqb):
        s = jnp.einsum('bqhd,bkhd->bhqk', qb, k_all).astype(jnp.float32)
        s = s + cqb.transpose(0, 2, 1)[..., None] - c_keys
        s = jnp.where(qp[:, None] >= kpos[None, :], s, NEG_INF)
        p = jax.nn.softmax(s, axis=-1).astype(v_all.dtype)
        return jnp.einsum('bhqk,bkhd->bqhd', p, v_all)

    y_b = _over_query_blocks(block, pos, q, c_q).reshape(B, T, FOX_W)
    out = jnp.concatenate([y_a, y_b], axis=-1) @ w_out
    return out, (k, v, logf.astype(h.dtype), h_last.astype(h.dtype), new_buf)

def _diff_mixer(h, pos, dk_past, dv_past, w_in, lam_params, subln_g, w_out, lam_init):
    B, T, _ = h.shape
    q, k, v = jnp.split(h @ w_in, 3, axis=-1)
    q = _rope(q.reshape(B, T, DIFF_HEADS, 2, DIFF_DH), pos) * (DIFF_DH ** -0.5)
    k = _rope(k.reshape(B, T, DIFF_HEADS, 2, DIFF_DH), pos)
    v = v.reshape(B, T, DIFF_HEADS, 2 * DIFF_DH)
    P = dk_past.shape[1]
    k_all = jnp.concatenate([dk_past.astype(k.dtype).reshape(B, P, DIFF_HEADS, 2, DIFF_DH), k], axis=1)
    v_all = jnp.concatenate([dv_past.astype(v.dtype), v], axis=1)
    lp = lam_params.astype(jnp.float32)
    lam = jnp.exp(jnp.sum(lp[0] * lp[1])) - jnp.exp(jnp.sum(lp[2] * lp[3])) + lam_init
    kchunk = jnp.arange(P + T, dtype=jnp.int32) // CHUNK

    def block(qp, qb):
        s = jnp.einsum('bqhcd,bkhcd->bhcqk', qb, k_all).astype(jnp.float32)
        s = jnp.where((qp // CHUNK)[:, None] >= kchunk[None, :], s, NEG_INF)
        p = jax.nn.softmax(s, axis=-1)
        a = (p[:, :, 0] - lam * p[:, :, 1]).astype(v_all.dtype)
        return jnp.einsum('bhqk,bkhd->bqhd', a, v_all)

    o = _over_query_blocks(block, pos, q)
    o = _rmsnorm(o, subln_g) * (1.0 - lam_init)
    out = o.reshape(B, T, DIFF_W) @ w_out
    return out, (k.reshape(B, T, DIFF_HEADS, 2 * DIFF_DH), v)

def _trunk(x, pos, fox_k, fox_v, fox_logf, lru_h, lru_conv, diff_k, diff_v,
           norm_g, w_ffn_in, w_ffn_out, w_in_even, b_fox_f, lru_conv_w, lru_conv_b,
           lru_w_gates, lru_b_gates, lru_lambda, w_out_even, w_in_odd, diff_lambda,
           diff_subln_g, w_out_odd):
    new_even, new_odd = [], []
    for l in range(DEPTH):
        g = norm_g[l]
        x = x + 0.5 * _rmsnorm(_swiglu(_rmsnorm(x, g[0]), w_ffn_in[l, 0], w_ffn_out[l, 0]), g[1])
        hn = _rmsnorm(x, g[2])
        if l % 2 == 0:
            e = l // 2
            m, st = _even_mixer(hn, pos, fox_k[e], fox_v[e], fox_logf[e], lru_h[e], lru_conv[e],
                                w_in_even[e], b_fox_f[e], lru_conv_w[e], lru_conv_b[e],
                                lru_w_gates[e], lru_b_gates[e], lru_lambda[e], w_out_even[e])
            new_even.append(st)
        else:
            o = l // 2
            lam_init = 0.8 - 0.6 * math.exp(-0.3 * l)
            m, st = _diff_mixer(hn, pos, diff_k[o], diff_v[o], w_in_odd[o], diff_lambda[o],
                                diff_subln_g[o], w_out_odd[o], lam_init)
            new_odd.append(st)
        x = x + _rmsnorm(m, g[3])
        x = x + 0.5 * _rmsnorm(_swiglu(_rmsnorm(x, g[4]), w_ffn_in[l, 1], w_ffn_out[l, 1]), g[5])
    even = [jnp.stack(z) for z in zip(*new_even)]
    odd = [jnp.stack(z) for z in zip(*new_odd)]
    return x, even, odd

def setup_inputs(seed: int = 0) -> dict:
    key = jax.random.key(seed)
    ks = jax.random.split(key, 24)
    nrm = jax.random.normal
    f32 = jnp.float32
    u = jax.random.uniform(ks[18], (N_EVEN, LRU_W), f32, 0.9, 0.999)
    s = u ** (1.0 / LRU_C)
    return {
        'x_prompt': nrm(ks[0], (BATCH, SEQ, D_MODEL), f32),
        'x_sample': nrm(ks[1], (DEC_BATCH, DEC_SEQ, D_MODEL), f32),
        'cache_fox_k': nrm(ks[2], (N_EVEN, DEC_BATCH, PAST_LEN, FOX_HEADS, FOX_DH), f32),
        'cache_fox_v': nrm(ks[3], (N_EVEN, DEC_BATCH, PAST_LEN, FOX_HEADS, FOX_DH), f32),
        'cache_fox_logf': jax.nn.log_sigmoid(2.0 + 0.5 * nrm(ks[4], (N_EVEN, DEC_BATCH, PAST_LEN, FOX_HEADS), f32)),
        'state_lru_h': 0.5 * nrm(ks[5], (N_EVEN, DEC_BATCH, LRU_W), f32),
        'state_lru_conv': nrm(ks[6], (N_EVEN, DEC_BATCH, CONV_W - 1, LRU_W), f32),
        'cache_diff_k': nrm(ks[7], (N_ODD, DEC_BATCH, PAST_LEN, DIFF_HEADS, 2 * DIFF_DH), f32),
        'cache_diff_v': nrm(ks[8], (N_ODD, DEC_BATCH, PAST_LEN, DIFF_HEADS, 2 * DIFF_DH), f32),
        'norm_g': 1.0 + 0.05 * nrm(ks[9], (DEPTH, 6, D_MODEL), f32),
        'w_ffn_in': nrm(ks[10], (DEPTH, 2, D_MODEL, 2 * D_FF), f32) * D_MODEL ** -0.5,
        'w_ffn_out': nrm(ks[11], (DEPTH, 2, D_FF, D_MODEL), f32) * D_FF ** -0.5,
        'w_in_even': nrm(ks[12], (N_EVEN, D_MODEL, EVEN_PROJ), f32) * D_MODEL ** -0.5,
        'b_fox_f': 2.0 + 0.5 * nrm(ks[13], (N_EVEN, FOX_HEADS), f32),
        'lru_conv_w': nrm(ks[14], (N_EVEN, CONV_W, LRU_W), f32) * CONV_W ** -0.5,
        'lru_conv_b': 0.01 * nrm(ks[15], (N_EVEN, LRU_W), f32),
        'lru_w_gates': nrm(ks[16], (N_EVEN, LRU_BLOCKS, LRU_BLOCK, 2 * LRU_BLOCK), f32) * LRU_BLOCK ** -0.5,
        'lru_b_gates': 0.01 * nrm(ks[17], (N_EVEN, LRU_BLOCKS, 2 * LRU_BLOCK), f32),
        'lru_lambda': jnp.log(s) - jnp.log1p(-s),
        'w_out_even': nrm(ks[19], (N_EVEN, EVEN_MIX_W, D_MODEL), f32) * EVEN_MIX_W ** -0.5,
        'w_in_odd': nrm(ks[20], (N_ODD, D_MODEL, 3 * DIFF_W), f32) * D_MODEL ** -0.5,
        'diff_lambda': 0.1 * nrm(ks[21], (N_ODD, 4, DIFF_DH), f32),
        'diff_subln_g': 1.0 + 0.05 * nrm(ks[22], (N_ODD, 2 * DIFF_DH), f32),
        'w_out_odd': nrm(ks[23], (N_ODD, DIFF_W, D_MODEL), f32) * DIFF_W ** -0.5,
    }

def reference(x_prompt, x_sample, cache_fox_k, cache_fox_v, cache_fox_logf, state_lru_h,
              state_lru_conv, cache_diff_k, cache_diff_v, norm_g, w_ffn_in, w_ffn_out,
              w_in_even, b_fox_f, lru_conv_w, lru_conv_b, lru_w_gates, lru_b_gates,
              lru_lambda, w_out_even, w_in_odd, diff_lambda, diff_subln_g, w_out_odd):
    weights = (norm_g, w_ffn_in, w_ffn_out, w_in_even, b_fox_f, lru_conv_w, lru_conv_b,
               lru_w_gates, lru_b_gates, lru_lambda, w_out_even, w_in_odd, diff_lambda,
               diff_subln_g, w_out_odd)
    B, S, _ = x_prompt.shape
    dt = x_prompt.dtype
    y_prompt, pe, po = _trunk(
        x_prompt, jnp.arange(S, dtype=jnp.int32),
        jnp.zeros((N_EVEN, B, 0, FOX_HEADS, FOX_DH), dt),
        jnp.zeros((N_EVEN, B, 0, FOX_HEADS, FOX_DH), dt),
        jnp.zeros((N_EVEN, B, 0, FOX_HEADS), dt),
        jnp.zeros((N_EVEN, B, LRU_W), dt),
        jnp.zeros((N_EVEN, B, CONV_W - 1, LRU_W), dt),
        jnp.zeros((N_ODD, B, 0, DIFF_HEADS, 2 * DIFF_DH), dt),
        jnp.zeros((N_ODD, B, 0, DIFF_HEADS, 2 * DIFF_DH), dt),
        *weights)
    past = cache_fox_k.shape[2]
    T = x_sample.shape[1]
    y_sample, se, so = _trunk(
        x_sample, past + jnp.arange(T, dtype=jnp.int32),
        cache_fox_k, cache_fox_v, cache_fox_logf, state_lru_h, state_lru_conv,
        cache_diff_k, cache_diff_v, *weights)
    p_fox_k, p_fox_v, p_fox_logf, p_lru_h, p_lru_conv = pe
    p_diff_k, p_diff_v = po
    s_fox_k, s_fox_v, s_fox_logf, s_lru_h, s_lru_conv = se
    s_diff_k, s_diff_v = so
    return (y_prompt, y_sample,
            p_fox_k, p_fox_v, p_fox_logf, p_lru_h, p_lru_conv, p_diff_k, p_diff_v,
            s_fox_k, s_fox_v, s_fox_logf, s_lru_h, s_lru_conv, s_diff_k, s_diff_v)


_drawn_inputs = setup_inputs


def setup_inputs(seed=0):
    import zlib

    import numpy as np

    out = dict(_drawn_inputs(seed))
    spreads = {}
    factors = {'lru_b_gates': 8.0}
    for name, (base, spread) in spreads.items():
        noise = np.random.default_rng([zlib.crc32(name.encode()), seed]).standard_normal(out[name].shape)
        drawn = base * np.exp(spread * noise) if base else spread * noise
        out[name] = jnp.asarray(drawn.astype(out[name].dtype))
    for name, factor in factors.items():
        out[name] = (out[name] * factor).astype(out[name].dtype)
    return out
```

```python
from contextlib import ExitStack

import concourse.bass as bass
from concourse import mybir

F32 = mybir.dt.float32
F32R = mybir.dt.float32r
ACT = mybir.ActivationFunctionType
ALU = mybir.AluOpType
AX = mybir.AxisListType

P = 128
EPS = 1e-6
D = 1024
KD = D // P
SEQ = 512
NS, TS = 8, 16
PAST = 128
TOK = SEQ + NS * TS
NT = TOK // P
NP = SEQ // P
FF = 2816
KF = FF // P
HALVES = [(0, 384), (384, 256)]
LW = 512
CL = LW // P
NH = 8
DH = 64
CW = 4
UP = CW - 1 + SEQ
US = CW - 1 + TS
UW = UP + NS * US
CHUNK = 64
NEG = -1e30
LAM_INIT = 0.8 - 0.6 * 2.718281828459045 ** -0.3
BW = 512
SLOT = BW + TOK

C_ID, C_UT, C_ONE, C_SL, C_NT, C_NC, C_UB = (i * P for i in (0, 1, 2, 5, 6, 7, 8))
C_COS = 9 * P
C_SIN = C_COS + NT * 8
C_NS = C_SIN + NT * 8
C_ALL = C_NS + TS

R_BUF, R_H0, R_CW, R_CB, R_LAM, R_BR, R_BI = 0, 24, 32, 36, 37, 38, 39
R_ALL = 40

UNITS = {}
_at = 0
for _name, _n in [("A0", 2 * KF), ("B0", 2 * KF), ("EG", 2 * CL), ("ET", 3 * KD), ("EO", 2 * KD),
                  ("A1", 2 * KF), ("B1", 2 * KF), ("A2", 2 * KF), ("B2", 2 * KF),
                  ("OT", 6 * KD), ("OO", 2 * KD), ("A3", 2 * KF), ("B3", 2 * KF)]:
    UNITS[_name] = _at
    _at += _n
RESULT = [(UNITS[_n], KD if _n[1] == "O" else KF) for _n in ("B0", "EO", "B1", "B2", "OO", "B3")]
CHUNKS = {"A0": 0, "EG": KF, "A1": KF + CL, "A2": 2 * KF + CL, "A3": 3 * KF + CL}
XT = {"pre0": 0, "pre1": 5, "yE": 10, "pre2": 15, "pre3": 20, "pre4": 25, "yO": 30, "pre5": 35}
READY = {"pre0": 0, "pre1": 5, "pre2": 10, "pre3": 15, "pre4": 20, "yO": 25, "pre5": 30}
GAIN_PRE = [(0, 0), (0, 2), (0, 4), (1, 0), (1, 2), (1, 4)]
GAIN_POST = [(0, 1), (0, 3), (0, 5), (1, 1), (1, 3), (1, 5)]
STEP = [0.5, 1.0, 0.5, 0.5, 1.0, 0.5]


def build_trunk(nc, a, o):
    ctx = ExitStack()
    with ctx:
        def sb(name, shape, dt=F32):
            return ctx.enter_context(nc.sbuf_tensor(name, shape, dt))

        def sem(name):
            return ctx.enter_context(nc.semaphore(name))

        x = sb("x", [P, NT, D])
        tok = sb("tok", [P, NT, D])
        xT_hi = sb("xT_hi", [P, KD, TOK], F32R)
        xT_lo = sb("xT_lo", [P, KD, TOK], F32R)
        raw = sb("raw", [P, 4, D])
        w_hi = sb("w_hi", [P, 2, SLOT], F32R)
        w_lo = sb("w_lo", [P, 2, SLOT], F32R)
        gain = sb("gain", [P, 2, D])
        arena = sb("arena", [P, 3 * NT * D])
        att = sb("att", [P, 3456])
        scratch = sb("scratch", [P, D])
        con = sb("con", [P, C_ALL])
        par = sb("par", [P, CL, R_ALL])
        small = sb("small", [P, 512])
        ps = ctx.enter_context(nc.psum_tensor("ps", [P, 8, 512], F32))
        psf = ps[:, :, :].rearrange("p b n -> p (b n)")

        def view(t, at, *dims):
            n = 1
            for d in dims:
                n *= d
            flat = t[:, at:at + n]
            if len(dims) == 1:
                return flat
            names = "abcd"[:len(dims)]
            return flat.rearrange("p (%s) -> p %s" % (" ".join(names), " ".join(names)),
                                  **{k: d for k, d in zip(names[1:], dims[1:])})

        hid = view(arena, 0, KF, TOK)
        silu = view(scratch, 0, 2, 384)
        ss_m, ss_x, rs_m, rs_x, vtmp = (view(small, 8 * i, 8) for i in range(5))
        nhalf = small[:, 40:41]
        lgf = view(small, 48, NT, NH)
        ls_all = small[:, 48:92]
        cl_a, cl_t = small[:, 92:96], small[:, 96:100]
        rmax, rneg, rsum, rinv = (view(small, 100 + 8 * i, 2, 4) for i in range(4))
        lamc = small[:, 132:136]
        bfb = small[:, 136:144]
        lsz, lst1, lst2, lst3 = (small[:, 144 + 44 * i:188 + 44 * i] for i in range(4))
        cq = view(small, 480, NP, NH)
        h0a = small[:, 320:328]
        s_ss = small[:, 464:472]
        s_rs = small[:, 472:480]
        ident = con[:, C_ID:C_ID + P]
        ones = con[:, C_ONE:C_ONE + P]

        raw_in = [sem("raw_in%d" % j) for j in range(4)]
        hi_done = sem("hi_done")
        lo_done = sem("lo_done")
        used = sem("used")
        a_mm = sem("a_mm")
        silu_done = sem("silu_done")
        h_done = sem("h_done")
        m_mm = sem("m_mm")
        m_out = sem("m_out")
        x_in, con_in, par_in = sem("x_in"), sem("con_in"), sem("par_in")
        gpost_in, gpre_in = sem("gpost_in"), sem("gpre_in")
        ss_m_done, ss_x_done = sem("ss_m_done"), sem("ss_x_done")
        rs_m_done, rs_x_done = sem("rs_m_done"), sem("rs_x_done")
        x_done = sem("x_done")
        tok_ready = sem("tok_ready")
        xt_ps = sem("xt_ps")
        xt_hi, xt_lo = sem("xt_hi"), sem("xt_lo")
        vs, ss_, gs = sem("vector_step"), sem("scalar_step"), sem("pool_step")
        t_mm, t_out = sem("t_mm"), sem("t_out")
        tr_mm, tr_out = sem("tr_mm"), sem("tr_out")
        rope_done = sem("rope_done")
        k_out, v_out = sem("k_out"), sem("v_out")
        f_mm, logf_done = sem("f_mm"), sem("logf_done")
        par_ps, par_done = sem("par_ps"), sem("par_done")
        wg_in = sem("wg_in")
        wf_hi_done, wf_lo_done = sem("wf_hi_done"), sem("wf_lo_done")
        e_abs, e_exp = sem("e_abs"), sem("e_exp")
        cq_mm, cq_done = sem("cq_mm"), sem("cq_done")
        conv_done, gate_mm = sem("conv_done"), sem("gate_mm")
        r_done, i_done, a_done, t_done = sem("r_done"), sem("i_done"), sem("a_done"), sem("t_done")
        m2_done, m_done = sem("m2_done"), sem("m_done")
        gz_done, gs_done, ya_done, ya_hi = sem("gz_done"), sem("gs_done"), sem("ya_done"), sem("ya_hi")
        hl_ready, hl_ps, hl_copied = sem("hl_ready"), sem("hl_ps"), sem("hl_copied")
        lru_end = sem("lru_end")
        out_sem = sem("y_stored")
        out_sem2 = sem("states_stored")
        subg_in = sem("subg_in")
        kc_in = [sem("kc_in0"), sem("kc_in1")]
        vc_in = [sem("vc_in0"), sem("vc_in1")]
        lf_in = sem("lf_in")
        kt_mm, kt_done = sem("kt_mm"), sem("kt_done")
        qb_done, ssc_mm, smax_done, sp_done = sem("qb_done"), sem("ssc_mm"), sem("smax_done"), sem("sp_done")
        sa_done, sat_mm, sat_done = sem("sa_done"), sem("sat_mm"), sem("sat_done")
        so_mm, so_done, sot_mm, sot_done = sem("so_mm"), sem("so_done"), sem("sot_mm"), sem("sot_done")
        lam_exp, lam_sum = sem("lam_exp"), sem("lam_sum")
        nc_mm, nc_done = sem("nc_mm"), sem("nc_done")
        qk_mm, s_read, s_ready, p_done, c_done = sem("qk_mm"), sem("s_read"), sem("s_ready"), sem("p_done"), sem("c_done")
        pt_mm, pt_done, pv_mm, o_done = sem("pt_mm"), sem("pt_done"), sem("pv_mm"), sem("o_done")
        sq_done, srs_done = sem("sq_done"), sem("srs_done")

        block = ctx.enter_context(nc.Block())

        u_pad = view(arena, 0, CL, UW)
        gate = view(arena, CL * UW, CL, TOK)
        at = CL * UW + CL * TOK
        vE = view(arena, at, NT, LW)
        qTE = view(arena, at + NT * LW, CL, TOK)
        kTE = view(arena, at + 2 * NT * LW, CL, TOK)
        at += 3 * NT * LW
        w_gate = view(arena, at, CL, 2, P)
        at += 2 * CL * P
        lfp = view(arena, at, NS, NH)
        prod = view(arena, at + 64, P)
        wf_hi = sb("wf_hi", [P, KD, NH], F32R)
        wf_lo = sb("wf_lo", [P, KD, NH], F32R)
        nlb = view(arena, at + 192, P)
        lfp_b = view(arena, at + 320, P)
        lgn = view(arena, at + 448, NT, NH)
        hl_rows = view(arena, at + 488, LW)
        prow = view(att, 0, LW)
        wf_raw = view(att, LW, KD, NH)
        lam_in = view(att, 576, 4, DH)
        lam_pr = view(att, 832, 2, DH)
        conv_c, r_c, i_c, t_c = (view(att, TOK * i, TOK) for i in range(4))
        g_c = view(att, 4 * TOK, TOK)
        hl = view(scratch, LW, CL, P)
        vO = view(arena, 0, NT, D)
        qTO = view(arena, NT * D, KD, TOK)
        kTO = view(arena, 2 * NT * D, KD, TOK)
        rot = [view(att, 640 * i, NT, 2 * NH, 8) for i in range(4)]
        sub_g = gain[:, 0, 0:P]
        negc = view(scratch, 0, 2, 512)
        stE = view(att, 0, 3, 512)
        ptE = view(att, 2048, 2, 4, P)
        pO = view(att, 0, 3, 2, 512)
        ptO = gain[:, 1, :].rearrange("p (a b c) -> p a b c", a=2, b=4)
        kts = [view(att, 1152 * i, KD, PAST + TS) for i in range(2)]
        qbd = view(att, 2304, D + P)
        s_sp = [view(att, 2944, 1, PAST + TS), gain[:, 1, 0:288].rearrange("p (m n) -> p m n", m=2)]
        s_sa = [att[:, 3088:3344], gain[:, 1, 288:544]]
        s_sat = [view(att, 576, 2, P), gain[:, 1, 544:800].rearrange("p (j n) -> p j n", j=2)]

        cosb = view(con, C_COS, NT, 8)
        sinb = view(con, C_SIN, NT, 8)

        def bank(b, n=512, at=0):
            return ps[:, b, at:at + n]

        def out_bank(n, t):
            return (5 * n + t) % 8

        def sp_unit(sp, u, it, src):
            if it is not None or u >= 4:
                sp.wait_ge(lo_done, (u - 3) + 4 * it if it is not None else u - 3)
            dst = raw[:, u % 4, 0:src.shape[-1]] if len(src.shape) == 2 else \
                raw[:, u % 4, :].rearrange("p (k n) -> p k n", n=P)
            sp.dma_start(dst, src).then_inc(raw_in[u % 4], 16)

        def sp_pairs(sp, name, w, stride, pairs):
            u0 = UNITS[name]
            wv = w.rearrange("(k p) n -> p k n", p=P)

            def some(c, it):
                for cc in range(2):
                    for which in range(2):
                        u = u0 + 2 * cc + which + 2 * c
                        if it is None:
                            src = wv[:, :, which * stride + (c + cc) * P:which * stride + (c + cc + 1) * P]
                        else:
                            src = wv[:, :, bass.ds(which * stride + cc * P + it * (2 * P), P)]
                        sp_unit(sp, u, it, src)
            some(0, None)
            with sp.Fori(1, pairs // 2, 1) as it:
                some(0, it)

        def sp_rows(sp, u0, w, blocks, rows):
            for b, c0 in enumerate(blocks):
                wb = w[:, c0:c0 + BW].rearrange("(k p) n -> p k n", p=P)
                full = rows // 4
                with sp.Fori(0, full, 1) as it:
                    for j in range(4):
                        u = u0 + b * rows + j
                        src = wb[:, bass.ds(it * 4 + j, 1), :].rearrange("p a n -> p (a n)")
                        sp_unit(sp, u, it, src)
                for k in range(4 * full, rows):
                    sp_unit(sp, u0 + b * rows + k, None, wb[:, k, :])

        def sp_ffn(sp, f):
            l, j = divmod(f, 2)
            sp_pairs(sp, "A%d" % f, a["w_ffn_in"][l, j], FF, KF)
            sp_rows(sp, UNITS["B%d" % f], a["w_ffn_out"][l, j], [0, BW], KF)

        def sp_caches(sp, odd):
            w = (1 + odd) * 512
            kc, vc = (a["cache_diff_k"], a["cache_diff_v"]) if odd else (a["cache_fox_k"], a["cache_fox_v"])
            for s in range(NS):
                if s == 0:
                    sp.wait_ge(lo_done, UNITS["OO"] if odd else UNITS["EO"])
                if s >= 2:
                    sp.wait_ge(kt_mm, NS * odd + s - 1)
                sp.dma_start(raw[:, s % 2, 0:w], kc[0, s].rearrange("t h d -> t (h d)")).then_inc(kc_in[s % 2], 16)
                if s >= 2:
                    sp.wait_ge(so_mm, NS * odd + s - 1)
                sp.dma_start(raw[:, 2 + s % 2, 0:w], vc[0, s].rearrange("t h d -> t (h d)")).then_inc(vc_in[s % 2], 16)
            sp.wait_ge(so_mm, NS * (odd + 1))

        @block.sync
        def _(sp):
            for t in range(NT):
                src = a["x_prompt"][0, t * P:(t + 1) * P, :] if t < NP else \
                    a["x_sample"].rearrange("s t d -> (s t) d")
                sp.dma_start(x[:, t, :], src).then_inc(x_in, 16)
            sp_ffn(sp, 0)
            sp_pairs(sp, "EG", a["w_in_even"][0], LW, CL)
            sp_rows(sp, UNITS["ET"], a["w_in_even"][0], [3 * LW, 2 * LW, 4 * LW], KD)
            sp_caches(sp, 0)
            sp_rows(sp, UNITS["EO"], a["w_out_even"][0], [0, BW], KD)
            sp_ffn(sp, 1)
            sp_ffn(sp, 2)
            sp_rows(sp, UNITS["OT"], a["w_in_odd"][0], [D, D + BW, 2 * D, 2 * D + BW, 0, BW], KD)
            sp_caches(sp, 1)
            sp_rows(sp, UNITS["OO"], a["w_out_odd"][0], [0, BW], KD)
            sp_ffn(sp, 3)
            for t in range(NT):
                sp.wait_ge(x_done, 5 * 5 + t + 1)
                dst = o["y_prompt"][0, t * P:(t + 1) * P, :] if t < NP else \
                    o["y_sample"].rearrange("s t d -> (s t) d")
                sp.dma_start(dst, x[:, t, :]).then_inc(out_sem, 16)
            sp.wait_ge(out_sem, 16 * NT)

        def act_hi(act, u, it, n):
            act.wait_ge(raw_in[u % 4], 16 * (u // 4 + 1) + (0 if it is None else 16 * it))
            if it is not None or u >= 2:
                act.wait_ge(used, u - 1 if it is None else (u - 1) + 4 * it)
            return nc.scalar.activation(w_hi[:, u % 2, 0:n], raw[:, u % 4, 0:n], ACT.Copy)

        def dve_lo(dve, u, it, n):
            dve.wait_ge(hi_done, u + 1 if it is None else (u + 1) + 4 * it)
            return nc.vector.tensor_tensor(w_lo[:, u % 2, 0:n], raw[:, u % 4, 0:n],
                                           w_hi[:, u % 2, 0:n].bitcast(F32), ALU.subtract)

        def at_chunk(k, it):
            return hid[:, k, :] if it is None else \
                hid[:, bass.ds(it * 4 + k, 1), :].rearrange("p a n -> p (a n)")

        def act_hi_b(act, u, it, k):
            act_hi(act, u, it, BW)
            nc.scalar.activation(w_hi[:, u % 2, BW:SLOT], at_chunk(k, it), ACT.Copy).then_inc(hi_done, 1)

        def dve_lo_b(dve, u, it, k):
            dve_lo(dve, u, it, BW)
            nc.vector.tensor_tensor(w_lo[:, u % 2, BW:SLOT], at_chunk(k, it),
                                    w_hi[:, u % 2, BW:SLOT].bitcast(F32), ALU.subtract).then_inc(lo_done, 1)

        def reg(base, it, per):
            return base if it is None else base + it * per

        def half_ready(eng, u0, c0, c, it, which, half):
            if half == 0:
                eng.wait_ge(a_mm, reg(2 * (c0 + c) + which + 1, it, 4))
            else:
                eng.wait_ge(used, reg(u0 + 2 * c + which + 1, it, 4))

        FFN_A = ["A0", "A1", "A2", "A3"]

        def act_ffn(act, f, tail):
            u0, c0, b0 = UNITS["A%d" % f], CHUNKS["A%d" % f], UNITS["B%d" % f]

            def gate_half(c, it, half):
                w = HALVES[half][1]
                half_ready(act, u0, c0, c, it, 0, half)
                if it is not None or c0 + c > 0:
                    act.wait_ge(h_done, reg(2 * (c0 + c - 1) + half + 1, it, 4))
                nc.scalar.activation(silu[:, half, 0:w], bank(4 * (c % 2) + half, w), ACT.Silu).then_inc(silu_done, 1)

            def chunk(c, it):
                act_hi(act, u0 + 2 * c + 2, it, D).then_inc(hi_done, 1)
                gate_half(c, it, 0)
                gate_half(c, it, 1)
                act_hi(act, u0 + 2 * c + 3, it, D).then_inc(hi_done, 1)

            chunk(0, None)
            chunk(1, None)
            with act.Fori(1, KF // 2 - 1, 1) as it:
                chunk(0, it)
                chunk(1, it)
            chunk(KF - 2, None)
            c = KF - 1
            act_hi_b(act, b0, None, 0)
            gate_half(c, None, 0)
            gate_half(c, None, 1)
            act.wait_ge(h_done, 2 * (c0 + KF))
            act_hi_b(act, b0 + 1, None, 1)
            for k in range(2, 4):
                act_hi_b(act, b0 + k, None, k)
            with act.Fori(1, KF // 4, 1) as it:
                for k in range(4):
                    act_hi_b(act, b0 + k, it, k)
            for k in range(4 * (KF // 4), KF):
                act_hi_b(act, b0 + k, None, k)
            for k in range(2):
                act_hi_b(act, b0 + KF + k, None, k)
            act_result(act, tail, 0)
            with act.Fori(0, KF // 4, 1) as it:
                for k in range(4):
                    act_hi_b(act, b0 + KF + 2 + k, it, k + 2)

        def dve_ffn(dve, f):
            u0, c0, b0 = UNITS["A%d" % f], CHUNKS["A%d" % f], UNITS["B%d" % f]

            def hidden_half(c, it, half):
                at0, w = HALVES[half]
                half_ready(dve, u0, c0, c, it, 1, half)
                dve.wait_ge(silu_done, reg(2 * (f * KF + c) + half + 1, it, 4))
                dst = hid[:, c, at0:at0 + w] if it is None else \
                    hid[:, bass.ds(it * 2 + c, 1), at0:at0 + w].rearrange("p a n -> p (a n)")
                nc.vector.tensor_tensor(dst, silu[:, half, 0:w], bank(4 * (c % 2) + 2 + half, w),
                                        ALU.mult).then_inc(h_done, 1)

            def chunk(c, it):
                dve_lo(dve, u0 + 2 * c + 2, it, D).then_inc(lo_done, 1)
                hidden_half(c, it, 0)
                hidden_half(c, it, 1)
                dve_lo(dve, u0 + 2 * c + 3, it, D).then_inc(lo_done, 1)

            chunk(0, None)
            chunk(1, None)
            with dve.Fori(1, KF // 2 - 1, 1) as it:
                chunk(0, it)
                chunk(1, it)
            chunk(KF - 2, None)
            c = KF - 1
            dve_lo_b(dve, b0, None, 0)
            hidden_half(c, None, 0)
            hidden_half(c, None, 1)
            dve.wait_ge(h_done, 2 * (c0 + KF))
            for k in range(1, 4):
                dve_lo_b(dve, b0 + k, None, k)
            with dve.Fori(1, KF // 4, 1) as it:
                for k in range(4):
                    dve_lo_b(dve, b0 + k, it, k)
            for k in range(4 * (KF // 4), KF):
                dve_lo_b(dve, b0 + k, None, k)
            for k in range(2):
                dve_lo_b(dve, b0 + KF + k, None, k)
            with dve.Fori(0, KF // 4, 1) as it:
                for k in range(4):
                    dve_lo_b(dve, b0 + KF + 2 + k, it, k + 2)

        def pe_pairs(pe, name, xt, chunks):
            u0, c0 = UNITS[name], CHUNKS[name]

            def chunk(c, it):
                for which in range(2):
                    u = u0 + 2 * c + which
                    pe.wait_ge(lo_done, reg(u + 1, it, 4))
                    for half in range(2):
                        at0, w = HALVES[half]
                        if it is None and c == 0 and which == 0:
                            pe.wait_ge(xt_lo, xt + (3, 5)[half])
                        if which == 0 and (it is not None or c0 + c >= 2):
                            pe.wait_ge(h_done, reg(2 * (c0 + c - 2) + half + 1, it, 4))
                        dst = bank(4 * (c % 2) + 2 * which + half, w)
                        for k in range(KD):
                            wh = w_hi[:, u % 2, k * P:(k + 1) * P]
                            wl = w_lo[:, u % 2, k * P:(k + 1) * P]
                            xh, xl = xT_hi[:, k, at0:at0 + w], xT_lo[:, k, at0:at0 + w]
                            nc.tensor.matmul(dst, wl, xh, start=(k == 0), stop=False)
                            nc.tensor.matmul(dst, wh, xl, start=False, stop=False)
                            mm = nc.tensor.matmul(dst, wh, xh, start=False, stop=(k == KD - 1))
                        mm.then_inc((a_mm, used)[half], 1)

            chunk(0, None)
            chunk(1, None)
            with pe.Fori(1, chunks // 2, 1) as it:
                chunk(0, it)
                chunk(1, it)

        def pe_row_unit(pe, u, it, k, lhs, banks, start, stop, before=None, done=None):
            pe.wait_ge(lo_done, reg(u + 1, it, 2))
            wh, wl = w_hi[:, u % 2, 0:BW], w_lo[:, u % 2, 0:BW]
            for t in range(NT):
                if before:
                    before(t)
                xh, xl = lhs(u, k, t)
                dst = bank(banks[t])
                nc.tensor.matmul(dst, xl, wh, start=start, stop=False)
                nc.tensor.matmul(dst, xh, wl, start=False, stop=False)
                mm = nc.tensor.matmul(dst, xh, wh, start=False, stop=stop)
                if done is not None and t < NT - 1:
                    mm.then_inc(done, 1)
            mm.then_inc(used, 1)

        def slot_lhs(u, k, t):
            at0 = BW + t * P
            return w_hi[:, u % 2, at0:at0 + P], w_lo[:, u % 2, at0:at0 + P]

        def xt_lhs(u, k, t):
            return xT_hi[:, k, t * P:(t + 1) * P], xT_lo[:, k, t * P:(t + 1) * P]

        def pe_ffn_out(pe, f, p):
            b0, c_end = UNITS["B%d" % f], CHUNKS["A%d" % f] + KF
            for n in range(2):
                banks = [out_bank(n, t) for t in range(NT)]
                u = b0 + n * KF

                def free(t):
                    if n == 0 and t in (0, 4):
                        pe.wait_ge(h_done, 2 * c_end - (2 if t == 0 else 0))
                    if n == 1 and banks[t] < 5:
                        pe.wait_ge(m_out, 10 * p + banks[t] + 1)

                pe_row_unit(pe, u, None, 0, slot_lhs, banks, True, False, before=free)
                pe_row_unit(pe, u + 1, None, 1, slot_lhs, banks, False, False)
                with pe.Fori(1, KF // 2 - 1, 1) as it:
                    pe_row_unit(pe, u, it, 0, slot_lhs, banks, False, False)
                    pe_row_unit(pe, u + 1, it, 1, slot_lhs, banks, False, False)
                pe_row_unit(pe, u + KF - 2, None, 0, slot_lhs, banks, False, False)
                pe_row_unit(pe, u + KF - 1, None, 1, slot_lhs, banks, False, True, done=m_mm)

        def act_result(act, p, n, tiles=range(NT)):
            for t in tiles:
                if t < NT - 1:
                    act.wait_ge(m_mm, 4 * (2 * p + n) + t + 1)
                else:
                    act.wait_ge(used, RESULT[p][0] + RESULT[p][1] * (n + 1))
                nc.scalar.activation(tok[:, t, n * BW:(n + 1) * BW], bank(out_bank(n, t)), ACT.Copy).then_inc(m_out, 1)

        last_square = []

        def act_norm(act, p, nxt=None):
            def square_after(done, count):
                if last_square:
                    act.wait_ge(*last_square.pop())
                last_square.append((done, count))

            def sq_m(t):
                act_result(act, p, 1, [t])
                act.wait_ge(m_out, 10 * p + 5 + t + 1)
                square_after(ss_m_done, 5 * p + t + 1)
                nc.scalar.activation(scratch[:, :], tok[:, t, :], ACT.Square,
                                     accum_out=ss_m[:, t:t + 1]).then_inc(ss_m_done, 1)

            def sq_x(t):
                if p >= 0:
                    act.wait_ge(x_done, 5 * p + t + 1)
                else:
                    act.wait_ge(x_in, 16 * NT)
                square_after(ss_x_done, 5 * (p + 1) + t + 1)
                nc.scalar.activation(scratch[:, :], x[:, t, :], ACT.Square,
                                     accum_out=ss_x[:, t:t + 1]).then_inc(ss_x_done, 1)

            for t in range(NT + 2):
                if t < NT and p >= 0:
                    sq_m(t)
                if p < 5:
                    if 1 <= t <= NT:
                        sq_x(t - 1)
                    if t >= 2:
                        act_xt(act, "pre%d" % (p + 1), t - 2, t - 2)
                if t == 3 and nxt:
                    for u in range(nxt[0], nxt[0] + 2):
                        act_hi(act, u, None, nxt[1]).then_inc(hi_done, 1)

        def pool_norm(pool, p):
            def inv(t, src, dst, ready, count, done):
                pool.wait_ge(ready, count)
                nc.gpsimd.tensor_scalar(vtmp[:, t:t + 1], src[:, t:t + 1], 1.0 / D, EPS, ALU.mult, ALU.add).then_inc(gs, 1)
                pool_count[0] += 1
                pool.wait_ge(gs, pool_count[0])
                nc.gpsimd.tensor_tensor(dst[:, t:t + 1], vtmp[:, t:t + 1], nhalf, ALU.pow).then_inc(done, 1)

            for t in range(NT + 1):
                if t < NT and p >= 0:
                    inv(t, ss_m, rs_m, ss_m_done, 5 * p + t + 1, rs_m_done)
                if t >= 1 and p < 5:
                    inv(t - 1, ss_x, rs_x, ss_x_done, 5 * (p + 1) + t, rs_x_done)

        def dve_norm(dve, p, nxt=None):
            def post(t):
                if t == 0:
                    dve.wait_ge(gpost_in, 16 * (p + 1))
                dve.wait_ge(rs_m_done, 5 * p + t + 1)
                link(dve, nc.vector.scalar_tensor_tensor(tok[:, t, :], tok[:, t, :], rs_m[:, t:t + 1], gain[:, 0, :],
                                                         ALU.mult, ALU.mult))
                nc.vector.scalar_tensor_tensor(x[:, t, :], tok[:, t, :], STEP[p], x[:, t, :],
                                               ALU.mult, ALU.add).then_inc(x_done, 1)

            def pre(t):
                if t == 0:
                    dve.wait_ge(gpre_in, 16 * (p + 2))
                dve.wait_ge(rs_x_done, 5 * (p + 1) + t + 1)
                nc.vector.scalar_tensor_tensor(tok[:, t, :], x[:, t, :], rs_x[:, t:t + 1], gain[:, 1, :],
                                               ALU.mult, ALU.mult).then_inc(tok_ready, 1)

            for t in range(NT + 2):
                if t < NT and p >= 0:
                    post(t)
                if p < 5:
                    if 1 <= t <= NT:
                        pre(t - 1)
                    if t >= 2:
                        dve_xt(dve, "pre%d" % (p + 1), t - 2, t - 2)
                if t == 3 and nxt:
                    for u in range(nxt[0], nxt[0] + 2):
                        dve_lo(dve, u, None, nxt[1]).then_inc(lo_done, 1)

        def xt_bank(i):
            return (2 + 2 * (i % 2)) * 512

        def pe_xt(pe, name, j, t, c0=0):
            i = XT[name] + j
            if name in READY:
                pe.wait_ge(tok_ready, READY[name] + j + 1)
            if i >= 2:
                pe.wait_ge(xt_lo, i - 1)
            for c in range(c0, KD):
                mm = nc.tensor.transpose(psf[:, xt_bank(i) + c * P:xt_bank(i) + (c + 1) * P],
                                         tok[:, t, c * P:(c + 1) * P], ident)
            mm.then_inc(xt_ps, 1)

        def xt_src(i, c0):
            return psf[:, xt_bank(i) + c0 * P:xt_bank(i) + D].rearrange("p (c n) -> p c n", n=P)

        def act_xt(act, name, j, t, c0=0):
            i = XT[name] + j
            act.wait_ge(xt_ps, i + 1)
            nc.scalar.activation(xT_hi[:, c0:KD, t * P:(t + 1) * P], xt_src(i, c0), ACT.Copy).then_inc(xt_hi, 1)

        def dve_xt(dve, name, j, t, c0=0):
            i = XT[name] + j
            dve.wait_ge(xt_hi, i + 1)
            nc.vector.tensor_tensor(xT_lo[:, c0:KD, t * P:(t + 1) * P], xt_src(i, c0),
                                    xT_hi[:, c0:KD, t * P:(t + 1) * P].bitcast(F32), ALU.subtract).then_inc(xt_lo, 1)

        def pool_gain_post(pool, p):
            if p:
                pool.wait_ge(x_done, 5 * p)
            if p == 4:
                pool.wait_ge(tok_ready, READY["yO"] + NT)
            pool.dma_start(gain[:, 0, :], a["norm_g"][GAIN_POST[p][0], GAIN_POST[p][1]].partition_broadcast(P))\
                .then_inc(gpost_in, 16)

        def pool_gain_pre(pool, p):
            if p:
                pool.wait_ge(tok_ready, READY["pre%d" % (p - 1)] + NT)
            if p == 5:
                pool.wait_ge(tok_ready, READY["yO"] + NT)
            pool.dma_start(gain[:, 1, :], a["norm_g"][GAIN_PRE[p][0], GAIN_PRE[p][1]].partition_broadcast(P))\
                .then_inc(gpre_in, 16)

        vcount, scount, pool_count = [0], [0], [0]

        def link(dve, ins):
            vcount[0] += 1
            ins.then_inc(vs, 1)
            dve.wait_ge(vs, vcount[0])

        def slink(act, ins):
            scount[0] += 1
            ins.then_inc(ss_, 1)
            act.wait_ge(ss_, scount[0])

        def pe_blocks(pe, name, first, blocks, t0, start=None):
            def one(b, it):
                def free(t):
                    if start and it is None:
                        start(t)
                    elif t0 or it is not None:
                        pe.wait_ge(t_out, reg(t0 + 5 * (b - 1) + t + 1, it, 5))
                for k in range(KD):
                    u = UNITS[name] + (first + b) * KD + k
                    pe.wait_ge(lo_done, reg(u + 1, it, KD))
                    wh, wl = w_hi[:, u % 2, 0:BW], w_lo[:, u % 2, 0:BW]
                    for t in range(NT):
                        if k == 0:
                            free(t)
                        xh, xl = xt_lhs(u, k, t)
                        nc.tensor.matmul(bank(t), xl, wh, start=(k == 0), stop=False)
                        nc.tensor.matmul(bank(t), xh, wl, start=False, stop=False)
                        mm = nc.tensor.matmul(bank(t), xh, wh, start=False, stop=(k == KD - 1))
                        if k == KD - 1 and t < NT - 1:
                            mm.then_inc(t_mm, 1)
                    mm.then_inc(used, 1)
            one(0, None)
            if blocks > 1:
                with pe.Fori(1, blocks, 1) as it:
                    one(0, it)

        def act_blocks(act, name, dests, t0, scales, before):
            for b in range(len(dests)):
                for k in range(2, KD + (2 if b + 1 < len(dests) else 0)):
                    act_hi(act, UNITS[name] + b * KD + k, None, BW).then_inc(hi_done, 1)
                before(b)
                for t in range(NT):
                    if t < NT - 1:
                        act.wait_ge(t_mm, 4 * (t0 // 5 + b) + t + 1)
                    else:
                        act.wait_ge(used, UNITS[name] + (b + 1) * KD)
                    nc.scalar.activation(dests[b](t), bank(t), ACT.Copy, scale=scales[b]).then_inc(t_out, 1)

        def dve_units(dve, u0, count):
            with dve.Fori(0, count // 4, 1) as it:
                for j in range(4):
                    dve_lo(dve, u0 + j, it, BW).then_inc(lo_done, 1)
            for j in range(4 * (count // 4), count):
                dve_lo(dve, u0 + j, None, BW).then_inc(lo_done, 1)

        def pe_tr(pe, i, src):
            if i >= 2:
                pe.wait_ge(tr_out, i - 1)
            for c in range(4):
                mm = nc.tensor.transpose(bank(5 + i % 2, P, c * P), src[:, c * P:(c + 1) * P], ident)
            mm.then_inc(tr_mm, 1)

        def dve_tr(dve, i, dst):
            dve.wait_ge(tr_mm, i + 1)
            nc.vector.tensor_copy(dst, bank(5 + i % 2).rearrange("p (c n) -> p c n", n=P)).then_inc(tr_out, 1)

        def pe_mix_out(pe, name, p, y):
            for n in range(2):
                banks = [out_bank(n, t) for t in range(NT)]

                def free(t):
                    if n == 0 and t == 0:
                        pe.wait_ge(xt_lo, XT[y] + NT)
                        if y == "yE":
                            pe.wait_ge(lru_end, CL)
                    if n == 1 and banks[t] < 5:
                        pe.wait_ge(m_out, 10 * p + banks[t] + 1)
                for k in range(KD):
                    u = UNITS[name] + n * KD + k
                    pe_row_unit(pe, u, None, k, xt_lhs, banks, k == 0, k == KD - 1,
                                before=free if k == 0 else None, done=m_mm if k == KD - 1 else None)

        def act_mix_out(act, name, p):
            u0 = UNITS[name]
            for i in range(KD + 2):
                act_hi(act, u0 + i, None, BW).then_inc(hi_done, 1)
            act_result(act, p, 0)
            for i in range(KD + 2, 2 * KD):
                act_hi(act, u0 + i, None, BW).then_inc(hi_done, 1)

        def kv(odd):
            return (kTO, vO, KD) if odd else (kTE, vE, CL)

        def s_banks(s):
            return 2 + 3 * (s % 2)

        def pe_sample(pe, odd):
            kT, v, n = kv(odd)
            sa, sat = s_sa[odd], s_sat[odd]
            w = P // n
            for s in range(NS + 1):
                g = NS * odd + s
                if s < NS:
                    pe.wait_ge(kc_in[s % 2], 16 * (NS // 2 * odd + s // 2 + 1))
                    if g:
                        pe.wait_ge(kt_done, g)
                    if s == 0:
                        pe.wait_ge(t_out, 15 + 30 * odd)
                        pe.wait_ge(tr_out, 10 + 20 * odd)
                        if not odd:
                            pe.wait_ge(i_done, CL)
                            pe.wait_ge(cq_done, 1)
                    for c in range(n):
                        mm = nc.tensor.transpose(psf[:, c * P:(c + 1) * P], raw[:, s % 2, c * P:(c + 1) * P], ident)
                    mm.then_inc(kt_mm, 1)
                    pe.wait_ge(kt_done, g + 1)
                    pe.wait_ge(qb_done, g + 1)
                    if s >= 2:
                        pe.wait_ge(sp_done, g - 1)
                    b = s_banks(s)
                    if odd:
                        for m in range(2):
                            for h in range(NH):
                                mm = nc.tensor.matmul(bank(b + m, PAST + TS),
                                                      qbd[64 * m:64 * m + 64, h * P:(h + 1) * P],
                                                      kts[s % 2][64 * m:64 * m + 64, h, :],
                                                      start=(h == 0), stop=(h == NH - 1))
                    else:
                        for at0, wk, lhs, rhs in ((0, PAST, lfp_b, con[:, C_SL:C_SL + PAST]),
                                                  (PAST, TS, nlb, con[:, C_UB + TS * s:C_UB + TS * (s + 1)])):
                            for c in range(CL):
                                nc.tensor.matmul(bank(b, wk, at0), qbd[:, c * P:(c + 1) * P],
                                                 kts[s % 2][:, c, at0:at0 + wk], start=(c == 0), stop=False)
                            nc.tensor.matmul(bank(b, wk, at0), lhs, rhs, start=False, stop=False)
                            mm = nc.tensor.matmul(bank(b, wk, at0), prod, ones[:, 0:wk], start=False, stop=True)
                    mm.then_inc(ssc_mm, 1)
                if s:
                    g, r = g - 1, s - 1
                    pe.wait_ge(sa_done, g + 1)
                    if g:
                        pe.wait_ge(sat_done, g)
                    for j in range(2):
                        mm = nc.tensor.transpose(bank(7, P, j * P), sa[:, j * P:(j + 1) * P], ident)
                    mm.then_inc(sat_mm, 1)
                    pe.wait_ge(sat_done, g + 1)
                    pe.wait_ge(vc_in[r % 2], 16 * (NS // 2 * odd + r // 2 + 1))
                    if g:
                        pe.wait_ge(so_done, g)
                    for c in range(n):
                        nc.tensor.matmul(bank(4, w, c * w), raw[:, 2 + r % 2, c * P:(c + 1) * P],
                                         sat[:, 0, c * w:(c + 1) * w], start=True, stop=False)
                        mm = nc.tensor.matmul(bank(4, w, c * w), v[:, NP, c * P:(c + 1) * P],
                                              sat[:, 1, c * w:(c + 1) * w], start=False, stop=True)
                    mm.then_inc(so_mm, 1)
            pe.wait_ge(so_done, NS * (odd + 1))
            for c in range(n):
                mm = nc.tensor.transpose(psf[:, 5 * 512 + c * P:5 * 512 + (c + 1) * P], view(scratch, c * P, P), ident)
            mm.then_inc(sot_mm, 1)

        def act_sample(act, odd):
            kT, v, n = kv(odd)
            sp_, sat = s_sp[odd], s_sat[odd]
            for s in range(NS + 1):
                g = NS * odd + s
                if s < NS:
                    act.wait_ge(kt_mm, g + 1)
                    if s >= 2:
                        act.wait_ge(ssc_mm, g - 1)
                    if s == 0:
                        act.wait_ge(rope_done if odd else lru_end, 2 if odd else CL)
                    nc.scalar.activation(kts[s % 2][:, 0:n, 0:PAST], psf[:, 0:n * P].rearrange("p (c t) -> p c t", t=PAST),
                                         ACT.Copy).then_inc(kt_done, 1)
                    act.wait_ge(smax_done, g + 1)
                    if g:
                        act.wait_ge(sa_done, g)
                    for m in range(1 + odd):
                        e = nc.scalar.activation(sp_[:, m, :], bank(s_banks(s) + m, PAST + TS), ACT.Exp,
                                                 bias=rneg[:, m, s % 2:s % 2 + 1], accum_out=rsum[:, m, s % 2:s % 2 + 1])
                    e.then_inc(sp_done, 1)
                if s:
                    g -= 1
                    act.wait_ge(sat_mm, g + 1)
                    if g:
                        act.wait_ge(so_mm, g)
                    nc.scalar.activation(sat, bank(7, 2 * P).rearrange("p (j n) -> p j n", j=2),
                                         ACT.Copy).then_inc(sat_done, 1)

        def dve_sample(dve, odd):
            kT, v, n = kv(odd)
            qT = qTO if odd else qTE
            sp_, sa = s_sp[odd], s_sa[odd]
            m = 1 + odd
            ot = view(scratch, 0, n, P)
            if not odd:
                dve.wait_ge(lf_in, 16)
                link(dve, nc.vector.tensor_scalar(nlb.rearrange("p (h q) -> p h q", q=TS),
                                                  lgf[:, NP, :].unsqueeze(2).to_broadcast([P, NH, TS]),
                                                  -1.0, None, ALU.mult))
            nc.vector.memset(qbd, 0.0) if odd else nc.vector.memset(qbd[:, 0:CL * P + P], 0.0)
            link(dve, nc.vector.memset(sa[:, P:2 * P], 0.0))

            def fill(s):
                g, q0 = NS * odd + s, SEQ + TS * s
                if g:
                    dve.wait_ge(ssc_mm, g)
                if odd:
                    nc.vector.tensor_copy(qbd[:, 0:NH * (P + TS)].rearrange("p (h x) -> p h x", x=P + TS)[:, :, 0:TS],
                                          qT[:, :, q0:q0 + TS])
                else:
                    for j in range(2):
                        nc.vector.tensor_copy(
                            qbd[64 * j:64 * j + 64, TS * j:TS * j + CL * (P + 2 * TS)]
                            .rearrange("p (c x) -> p c x", x=P + 2 * TS)[:, :, 0:TS],
                            qT[64 * j:64 * j + 64, :, q0:q0 + TS])
                    nc.vector.tensor_tensor(prod.rearrange("p (h q) -> p h q", q=TS),
                                            lgf[:, NP, :].unsqueeze(2).to_broadcast([P, NH, TS]),
                                            con[:, C_UB + TS * s:C_UB + TS * (s + 1)].unsqueeze(1).to_broadcast([P, NH, TS]),
                                            ALU.mult)
                    nc.vector.tensor_copy(lfp_b.rearrange("p (h q) -> p h q", q=TS),
                                          lfp[:, s, :].unsqueeze(2).to_broadcast([P, NH, TS]))
                nc.vector.tensor_copy(kts[s % 2][:, 0:n, PAST:PAST + TS], kT[:, :, q0:q0 + TS]).then_inc(qb_done, 1)

            def softmax(s):
                g, b, j = NS * odd + s, s_banks(s), s % 2
                dve.wait_ge(ssc_mm, g + 1)
                if not odd:
                    link(dve, nc.vector.tensor_tensor(bank(b, TS, PAST), bank(b, TS, PAST), con[:, C_NS:C_NS + TS], ALU.add))
                link(dve, nc.vector.tensor_reduce(rmax[:, 0:m, j:j + 1], ps[:, b:b + m, 0:PAST + TS], AX.X, ALU.max))
                nc.vector.tensor_scalar(rneg[:, 0:m, j:j + 1], rmax[:, 0:m, j:j + 1], -1.0, None, ALU.mult).then_inc(smax_done, 1)

            def normalize(s):
                g, j = NS * odd + s, s % 2
                dve.wait_ge(sp_done, g + 1)
                link(dve, nc.vector.reciprocal(rinv[:, 0:m, j:j + 1], rsum[:, 0:m, j:j + 1]))
                if s:
                    dve.wait_ge(sat_mm, g)
                    nc.vector.memset(sa[:, P + TS * (s - 1):P + TS * s], 0.0)
                mine = sa[:, P + TS * s:P + TS * (s + 1)]
                if odd:
                    link(dve, nc.vector.tensor_scalar(sp_[:, 1, :], sp_[:, 1, :], rinv[:, 1, j:j + 1], lamc[:, 1:2],
                                                      ALU.mult, ALU.mult))
                    nc.vector.scalar_tensor_tensor(sa[:, 0:P], sp_[:, 0, 0:P], rinv[:, 0, j:j + 1], sp_[:, 1, 0:P],
                                                   ALU.mult, ALU.add)
                    nc.vector.scalar_tensor_tensor(mine, sp_[:, 0, P:P + TS], rinv[:, 0, j:j + 1], sp_[:, 1, P:P + TS],
                                                   ALU.mult, ALU.add).then_inc(sa_done, 1)
                else:
                    nc.vector.tensor_scalar(sa[:, 0:P], sp_[:, 0, 0:P], rinv[:, 0, j:j + 1], None, ALU.mult)
                    nc.vector.tensor_scalar(mine, sp_[:, 0, P:P + TS], rinv[:, 0, j:j + 1], None,
                                            ALU.mult).then_inc(sa_done, 1)

            def out(s):
                dve.wait_ge(so_mm, NS * odd + s + 1)
                if odd:
                    nc.vector.tensor_copy(ot[:, :, TS * s:TS * (s + 1)],
                                          bank(4, P).rearrange("p (h q) -> p h q", q=TS)).then_inc(so_done, 1)
                else:
                    for j in range(2):
                        oc = nc.vector.tensor_copy(ot[64 * j:64 * j + 64, :, TS * s:TS * (s + 1)],
                                                   ps[64 * j:64 * j + 64, 4, 0:P]
                                                   .rearrange("p (c x) -> p c x", x=2 * TS)[:, :, TS * j:TS * (j + 1)])
                    oc.then_inc(so_done, 1)

            fill(0)
            for s in range(NS):
                softmax(s)
                if s + 1 < NS:
                    fill(s + 1)
                if s:
                    out(s - 1)
                normalize(s)
            out(NS - 1)
            dve.wait_ge(sot_mm, odd + 1)
            dve.wait_ge(k_out, 32 * (odd + 1))
            dve.wait_ge(v_out, 32 * (odd + 1))
            dst = tok[:, NP, :] if odd else tok[:, NP, LW:D]
            nc.vector.tensor_copy(dst, psf[:, 5 * 512:5 * 512 + n * P]).then_inc(sot_done, 1)

        def steps(odd):
            if odd:
                return [(i * NH + h, i, h) for i in range(NP) for h in range(NH)]
            return [(h * NP + i, i, h) for h in range(NH) for i in range(NP)]

        NSTEP = NP * NH

        def sc_bank(n, odd):
            return 2 * (n % 2) if odd else (0, 1, 7)[n % 3]

        def pe_prompt(pe, odd):
            st = steps(odd)
            g0 = NSTEP * odd
            for j in range(NSTEP + 3):
                if j < NSTEP:
                    n, i, h = st[j]
                    g = g0 + n
                    w = (i + 1) * P
                    if n == 0:
                        pe.wait_ge(sot_done, odd + 1)
                        if not odd:
                            pe.wait_ge(hl_copied, 1)
                    if not odd:
                        if i == 0:
                            if h:
                                pe.wait_ge(nc_done, h)
                            for kb in range(NP):
                                for b in range(kb + 1):
                                    mm = nc.tensor.matmul(bank(6, P, kb * P), lgn[:, b, h:h + 1].to_broadcast([P, P]),
                                                          con[:, C_UT:C_UT + P] if b == kb else ones,
                                                          start=(b == 0), stop=(b == kb))
                            mm.then_inc(nc_mm, 1)
                        if n >= 3:
                            pe.wait_ge(s_read, g - 2)
                        c, pb = h // 2, 64 * (h % 2)
                        mm = nc.tensor.matmul(bank(sc_bank(n, odd), w), qTE[pb:pb + 64, c, i * P:(i + 1) * P],
                                              kTE[pb:pb + 64, c, 0:w], start=True, stop=True)
                    else:
                        if n >= 2:
                            pe.wait_ge(p_done, g - 1)
                        for m in range(2):
                            mm = nc.tensor.matmul(bank(sc_bank(n, odd) + m, w), qTO[64 * m:64 * m + 64, h, i * P:(i + 1) * P],
                                                  kTO[64 * m:64 * m + 64, h, 0:w], start=True, stop=True)
                    mm.then_inc(qk_mm, 1)
                if 2 <= j < NSTEP + 2:
                    n, i, h = st[j - 2]
                    g = g0 + n
                    pe.wait_ge(c_done if odd else p_done, g + 1)
                    if n >= 2:
                        pe.wait_ge(pt_done, g - 1)
                    b = (4 if odd else 2) + n % 2
                    src = pO[:, n % 3, 0, :] if odd else stE[:, n % 3, :]
                    for kb in range(i + 1):
                        mm = nc.tensor.transpose(bank(b, P, kb * P), src[:, kb * P:(kb + 1) * P], ident)
                    mm.then_inc(pt_mm, 1)
                if j >= 3:
                    n, i, h = st[j - 3]
                    g = g0 + n
                    pe.wait_ge(pt_done, g + 1)
                    if n >= 2:
                        pe.wait_ge(o_done, g - 1)
                    b = (6 if odd else 4) + n % 2
                    pt = (ptO if odd else ptE)[:, n % 2]
                    w = P if odd else DH
                    v = vO if odd else vE
                    for kb in range(i + 1):
                        mm = nc.tensor.matmul(bank(b, w), pt[:, kb, :], v[:, kb, h * w:(h + 1) * w],
                                              start=(kb == 0), stop=(kb == i))
                    mm.then_inc(pv_mm, 1)

        def act_prompt(act, odd):
            st = steps(odd)
            g0 = NSTEP * odd
            for j in range(NSTEP + 2):
                if j < NSTEP:
                    n, i, h = st[j]
                    g = g0 + n
                    w = (i + 1) * P
                    if not odd and i == 0:
                        act.wait_ge(nc_mm, h + 1)
                        if h >= 2:
                            act.wait_ge(s_read, NP * (h - 1))
                        elif h == 0:
                            act.wait_ge(sot_done, 1)
                        nc.scalar.activation(negc[:, h % 2, :], bank(6), ACT.Copy).then_inc(nc_done, 1)
                    act.wait_ge(s_ready, g + 1)
                    r = slice(n % 4, n % 4 + 1)
                    if odd:
                        if n >= 3:
                            act.wait_ge(pt_mm, g - 2)
                        elif n == 0:
                            act.wait_ge(sot_done, 2)
                        for m in range(2):
                            e = nc.scalar.activation(pO[:, n % 3, m, 0:w], bank(sc_bank(n, odd) + m, w), ACT.Exp,
                                                     bias=rneg[:, m, r], accum_out=rsum[:, m, r])
                    else:
                        e = nc.scalar.activation(stE[:, n % 3, 0:w], stE[:, n % 3, 0:w], ACT.Exp,
                                                 bias=rneg[:, 0, r], accum_out=rsum[:, 0, r])
                    e.then_inc(p_done, 1)
                if j >= 2:
                    n, i, h = st[j - 2]
                    g = g0 + n
                    act.wait_ge(pt_mm, g + 1)
                    if n >= 2:
                        act.wait_ge(pv_mm, g - 1)
                    w = (i + 1) * P
                    pt = (ptO if odd else ptE)[:, n % 2, 0:i + 1, :]
                    nc.scalar.activation(pt, bank((4 if odd else 2) + n % 2, w).rearrange("p (k n) -> p k n", n=P),
                                         ACT.Copy).then_inc(pt_done, 1)

        def dve_prompt(dve, odd):
            st = steps(odd)
            g0 = NSTEP * odd

            def scores(n, i, h):
                g, w = g0 + n, (i + 1) * P
                r = slice(n % 4, n % 4 + 1)
                dve.wait_ge(qk_mm, g + 1)
                if odd:
                    b = sc_bank(n, odd)
                    both = ps[:, b:b + 2, i * P:w]
                    link(dve, nc.vector.tensor_tensor(both, both, con[:, C_NC:C_NC + P].unsqueeze(1).to_broadcast([P, 2, P]), ALU.add))
                    link(dve, nc.vector.tensor_reduce(rmax[:, :, r], ps[:, b:b + 2, 0:w], AX.X, ALU.max))
                    nc.vector.tensor_scalar(rneg[:, :, r], rmax[:, :, r], -1.0, None, ALU.mult).then_inc(s_ready, 1)
                    return
                if i == 0:
                    dve.wait_ge(nc_done, h + 1)
                if n >= 3:
                    dve.wait_ge(pt_mm, g - 2)
                s_t = stE[:, n % 3, :]
                nc.vector.scalar_tensor_tensor(s_t[:, 0:w], bank(sc_bank(n, odd), w), cq[:, i, h:h + 1],
                                               negc[:, h % 2, 0:w], ALU.add, ALU.add).then_inc(s_read, 1)
                dve.wait_ge(s_read, g + 1)
                link(dve, nc.vector.tensor_tensor(s_t[:, i * P:w], s_t[:, i * P:w], con[:, C_NT:C_NT + P], ALU.add))
                link(dve, nc.vector.tensor_reduce(rmax[:, 0, r], s_t[:, 0:w], AX.X, ALU.max))
                nc.vector.tensor_scalar(rneg[:, 0, r], rmax[:, 0, r], -1.0, None, ALU.mult).then_inc(s_ready, 1)

            def combine(n, i, h):
                g, w = g0 + n, (i + 1) * P
                r = slice(n % 4, n % 4 + 1)
                dve.wait_ge(p_done, g + 1)
                if not odd:
                    nc.vector.reciprocal(rinv[:, 0, r], rsum[:, 0, r]).then_inc(c_done, 1)
                    return
                p1, p2 = pO[:, n % 3, 0, 0:w], pO[:, n % 3, 1, 0:w]
                link(dve, nc.vector.reciprocal(rinv[:, :, r], rsum[:, :, r]))
                link(dve, nc.vector.tensor_scalar(p2, p2, rinv[:, 1, r], lamc[:, 1:2], ALU.mult, ALU.mult))
                nc.vector.scalar_tensor_tensor(p1, p1, rinv[:, 0, r], p2, ALU.mult, ALU.add).then_inc(c_done, 1)

            def out(n, i, h):
                g = g0 + n
                dve.wait_ge(pv_mm, g + 1)
                if odd:
                    nc.vector.tensor_copy(tok[:, i, h * P:(h + 1) * P], bank(6 + n % 2, P)).then_inc(o_done, 1)
                else:
                    dve.wait_ge(c_done, g + 1)
                    nc.vector.tensor_scalar(tok[:, i, LW + h * DH:LW + (h + 1) * DH], bank(4 + n % 2, DH),
                                            rinv[:, 0, n % 4:n % 4 + 1], None, ALU.mult).then_inc(o_done, 1)

            if odd:
                dve_subnorm(dve, NP)
            for j in range(NSTEP + 3):
                if j < NSTEP:
                    scores(*st[j])
                if 1 <= j <= NSTEP:
                    combine(*st[j - 1])
                if j >= 3:
                    out(*st[j - 3])
                    if odd and (j - 2) % NH == 0:
                        dve_subnorm(dve, (j - 2) // NH - 1)

        def dve_subnorm(dve, t):
            if t < NP:
                dve.wait_ge(o_done, NSTEP + (t + 1) * NH)
            else:
                dve.wait_ge(sot_done, 2)
            k = (t + 1) % NT
            if k == 0:
                dve.wait_ge(subg_in, 16)
            sq = scratch[:, :]
            link(dve, nc.vector.tensor_tensor(sq, tok[:, t, :], tok[:, t, :], ALU.mult))
            nc.vector.tensor_reduce(s_ss, sq.rearrange("p (h d) -> p h d", d=P), AX.X, ALU.add).then_inc(sq_done, 1)
            dve.wait_ge(srs_done, k + 1)
            heads = tok[:, t, :].rearrange("p (h d) -> p h d", d=P)
            link(dve, nc.vector.tensor_tensor(heads, heads, s_rs.unsqueeze(2).to_broadcast([P, NH, P]), ALU.mult))
            nc.vector.scalar_tensor_tensor(heads, heads, 1.0 - LAM_INIT, sub_g.unsqueeze(1).to_broadcast([P, NH, P]),
                                           ALU.mult, ALU.mult).then_inc(tok_ready, 1)

        def lru_u(c, j):
            return (u_pad[:, c, j:j + SEQ],
                    u_pad[:, c, UP:UW].rearrange("p (s x) -> p s x", x=US)[:, :, j:j + TS])

        def samples(t):
            return t[:, SEQ:TOK].rearrange("p (s x) -> p s x", x=TS)

        def dve_even_pairs(dve):
            u0, c0 = UNITS["EG"], CHUNKS["EG"]
            nc.vector.memset(u_pad[:, :, 0:CW - 1], 0.0)
            for c in range(CL):
                nc.vector.tensor_copy(u_pad[:, c, UP:UW].rearrange("p (s x) -> p s x", x=US)[:, :, 0:CW - 1],
                                      par[:, c, R_BUF:R_BUF + 24].rearrange("p (s x) -> p s x", x=CW - 1))
            for c in range(CL):
                n = D if c + 1 < CL else BW
                dve_lo(dve, u0 + 2 * c + 2, None, n).then_inc(lo_done, 1)
                for half in range(2):
                    at0, w = HALVES[half]
                    half_ready(dve, u0, c0, c, None, 0, half)
                    wp = min(at0 + w, SEQ) - at0
                    nc.vector.tensor_copy(u_pad[:, c, CW - 1 + at0:CW - 1 + at0 + wp], bank(4 * (c % 2) + half, wp))
                    if wp < w:
                        nc.vector.tensor_copy(lru_u(c, CW - 1)[1], bank(4 * (c % 2) + half, w - wp, wp)
                                              .rearrange("p (s x) -> p s x", x=TS))
                for half in range(2):
                    at0, w = HALVES[half]
                    half_ready(dve, u0, c0, c, None, 1, half)
                    nc.vector.tensor_copy(gate[:, c, at0:at0 + w], bank(4 * (c % 2) + 2 + half, w)).then_inc(h_done, 1)
                dve_lo(dve, u0 + 2 * c + 3, None, n).then_inc(lo_done, 1)

        def act_even_pairs(act):
            for c in range(CL):
                n = D if c + 1 < CL else BW
                for j in range(2):
                    act_hi(act, UNITS["EG"] + 2 * c + 2 + j, None, n).then_inc(hi_done, 1)

        def pe_forget(pe):
            pe.wait_ge(wf_lo_done, 1)
            for t in range(NT):
                for k in range(KD):
                    xh, xl = xt_lhs(0, k, t)
                    dst = bank(7, NH, t * NH)
                    nc.tensor.matmul(dst, xl, wf_hi[:, k, :], start=(k == 0), stop=False)
                    nc.tensor.matmul(dst, xh, wf_lo[:, k, :], start=False, stop=False)
                    mm = nc.tensor.matmul(dst, xh, wf_hi[:, k, :], start=False, stop=(k == KD - 1))
            mm.then_inc(f_mm, 1)

        def pe_cumulate(pe):
            pe.wait_ge(logf_done, 1)
            for i in range(NP):
                for b in range(i + 1):
                    mm = nc.tensor.matmul(bank(7, NH, 64 + i * NH), con[:, C_UT:C_UT + P] if b == i else ones,
                                          lgf[:, b, :], start=(b == 0), stop=(b == i))
            mm.then_inc(cq_mm, 1)

        def dve_forget(dve):
            dve.wait_ge(f_mm, 1)
            nc.vector.tensor_tensor(lsz[:, 0:NT * NH].rearrange("p (t h) -> p t h", h=NH),
                                    bank(7, NT * NH).rearrange("p (t h) -> p t h", h=NH),
                                    bfb.unsqueeze(1).to_broadcast([P, NT, NH]), ALU.add)
            link(dve, nc.vector.tensor_copy(lsz[:, NT * NH:].unsqueeze(2), par[:, :, R_LAM:R_LAM + 1]))
            link(dve, nc.vector.tensor_scalar(lst1, lsz, -1.0, None, ALU.mult))
            nc.vector.tensor_tensor(lst1, lsz, lst1, ALU.max).then_inc(e_abs, 1)
            dve.wait_ge(e_exp, 1)
            link(dve, nc.vector.tensor_scalar(lst1, lst2, 2.0, None, ALU.add))
            link(dve, nc.vector.reciprocal(lst1, lst1))
            link(dve, nc.vector.tensor_tensor(lst1, lst2, lst1, ALU.mult))
            link(dve, nc.vector.tensor_tensor(lst3, lst1, lst1, ALU.mult))
            link(dve, nc.vector.tensor_scalar(lst2, lst3, 1.0 / 17, None, ALU.mult))
            for k in range(15, 1, -2):
                link(dve, nc.vector.scalar_tensor_tensor(lst2, lst2, 1.0 / k, lst3, ALU.add, ALU.mult))
            nc.vector.tensor_scalar(lst3, lsz, 0.0, None, ALU.min)
            link(dve, nc.vector.scalar_tensor_tensor(lst2, lst2, 1.0, lst1, ALU.add, ALU.mult))
            link(dve, nc.vector.scalar_tensor_tensor(ls_all, lst2, -2.0, lst3, ALU.mult, ALU.add))
            nc.vector.tensor_scalar(cl_a, ls_all[:, NT * NH:], 8.0, None, ALU.mult)
            nc.vector.tensor_scalar(cl_t, ls_all[:, NT * NH:], -8.0, None, ALU.mult)
            nc.vector.tensor_scalar(lgn, lgf, -1.0, None, ALU.mult).then_inc(logf_done, 1)
            dve.wait_ge(cq_mm, 1)
            nc.vector.tensor_copy(cq, bank(7, NP * NH, 64).rearrange("p (t h) -> p t h", h=NH)).then_inc(cq_done, 1)

        def pe_gates(pe, c):
            pe.wait_ge(conv_done, c + 1)
            if c == 0:
                pe.wait_ge(wg_in, 64)
                pe.wait_ge(t_out, 15)
            else:
                pe.wait_ge(i_done, c)
            for j in range(2):
                nc.tensor.matmul(bank(2 * j), w_gate[:, c, j, :], conv_c[:, 0:SEQ], start=True, stop=True)
                mm = nc.tensor.matmul(bank(2 * j + 1, TOK - SEQ), w_gate[:, c, j, :], conv_c[:, SEQ:TOK],
                                      start=True, stop=True)
            mm.then_inc(gate_mm, 1)

        def act_lru(act, c):
            act.wait_ge(gate_mm, c + 1)
            if c:
                act.wait_ge(ya_done, c)
            nc.scalar.activation(r_c, psf[:, 0:TOK], ACT.Sigmoid, bias=par[:, c, R_BR:R_BR + 1]).then_inc(r_done, 1)
            nc.scalar.activation(i_c, psf[:, 2 * 512:2 * 512 + TOK], ACT.Sigmoid,
                                 bias=par[:, c, R_BI:R_BI + 1]).then_inc(i_done, 1)
            act.wait_ge(gz_done, c + 1)
            nc.scalar.activation(g_c, g_c, ACT.Sigmoid, scale=1.5957691216057308).then_inc(gs_done, 1)
            act.wait_ge(r_done, c + 1)
            if c == 0:
                act.wait_ge(logf_done, 1)
            nc.scalar.activation(t_c, r_c, ACT.Tanh, scale=cl_t[:, c:c + 1]).then_inc(t_done, 1)
            act.wait_ge(t_done, c + 1)
            nc.scalar.activation(r_c, r_c, ACT.Exp, scale=cl_a[:, c:c + 1]).then_inc(a_done, 1)
            act.wait_ge(m2_done, c + 1)
            nc.scalar.activation(t_c, t_c, ACT.Sqrt).then_inc(m_done, 1)
            act.wait_ge(ya_done, c + 1)
            if c == 0:
                act.wait_ge(used, UNITS["ET"] + 3 * KD)
                act.wait_ge(f_mm, 1)
            nc.scalar.activation(xT_hi[:, c, :], gate[:, c, :], ACT.Copy).then_inc(ya_hi, 1)

        def dve_lru(dve, c):
            up, us = lru_u(c, 0)
            cp, cs = conv_c[:, 0:SEQ], samples(conv_c)
            if c:
                dve.wait_ge(gate_mm, c)
            w0, b0 = par[:, c, R_CW:R_CW + 1], par[:, c, R_CB:R_CB + 1]
            nc.vector.tensor_scalar(cp, up, w0, b0, ALU.mult, ALU.add)
            link(dve, nc.vector.tensor_scalar(cs, us, w0, b0, ALU.mult, ALU.add))
            for j in range(1, CW):
                up, us = lru_u(c, j)
                wj = par[:, c, R_CW + j:R_CW + j + 1]
                nc.vector.scalar_tensor_tensor(cp, up, wj, cp, ALU.mult, ALU.add)
                step = nc.vector.scalar_tensor_tensor(cs, us, wj, cs, ALU.mult, ALU.add)
                if j < CW - 1:
                    link(dve, step)
            step.then_inc(conv_done, 1)
            g = gate[:, c, :]
            link(dve, nc.vector.tensor_tensor(g_c, g, g, ALU.mult))
            link(dve, nc.vector.tensor_scalar(g_c, g_c, 0.044715, 1.0, ALU.mult, ALU.add))
            nc.vector.tensor_tensor(g_c, g_c, g, ALU.mult).then_inc(gz_done, 1)
            dve.wait_ge(i_done, c + 1)
            dve.wait_ge(conv_done, c + 1)
            link(dve, nc.vector.tensor_tensor(i_c, i_c, conv_c, ALU.mult))
            dve.wait_ge(t_done, c + 1)
            link(dve, nc.vector.tensor_scalar(conv_c, t_c, 1.0, None, ALU.add))
            link(dve, nc.vector.reciprocal(conv_c, conv_c))
            nc.vector.scalar_tensor_tensor(t_c, t_c, 2.0, conv_c, ALU.mult, ALU.mult).then_inc(m2_done, 1)
            dve.wait_ge(gs_done, c + 1)
            link(dve, nc.vector.tensor_tensor(g_c, g_c, g, ALU.mult))
            dve.wait_ge(m_done, c + 1)
            dve.wait_ge(a_done, c + 1)
            nc.vector.tensor_tensor(i_c, i_c, t_c, ALU.mult)
            first_a, first_b = samples(r_c)[:, :, 0:1], samples(i_c)[:, :, 0:1]
            link(dve, nc.vector.tensor_tensor(h0a.unsqueeze(2), first_a, par[:, c, R_H0:R_H0 + NS].unsqueeze(2), ALU.mult))
            nc.vector.tensor_tensor(first_b, first_b, h0a.unsqueeze(2), ALU.add)
            link(dve, nc.vector.memset(first_a, 0.0))
            link(dve, nc.vector.tensor_tensor_scan(t_c, r_c, i_c, 0.0, ALU.mult, ALU.add))
            nc.vector.tensor_copy(hl[:, c, 0:1], t_c[:, SEQ - 1:SEQ])
            nc.vector.tensor_copy(hl[:, c, 1:9].unsqueeze(2), samples(t_c)[:, :, TS - 1:TS])
            nc.vector.tensor_copy(hl[:, c, 9:12], u_pad[:, c, SEQ:UP])
            nc.vector.tensor_copy(hl[:, c, 12:36].rearrange("p (s x) -> p s x", x=CW - 1),
                                  u_pad[:, c, UP:UW].rearrange("p (s x) -> p s x", x=US)[:, :, TS:US]).then_inc(hl_ready, 1)
            nc.vector.tensor_tensor(gate[:, c, :], t_c, g_c, ALU.mult).then_inc(ya_done, 1)
            dve.wait_ge(ya_hi, c + 1)
            dve.wait_ge(ya_done, c + 1)
            nc.vector.tensor_tensor(xT_lo[:, c, :], gate[:, c, :], xT_hi[:, c, :].bitcast(F32),
                                    ALU.subtract).then_inc(lru_end, 1)

        def pe_last_rows(pe):
            pe.wait_ge(hl_ready, CL)
            for c in range(CL):
                mm = nc.tensor.transpose(bank(7, P, c * P), hl[:, c, :], ident)
            mm.then_inc(hl_ps, 1)

        def rope(dve, k):
            xs = tok[:, :, :].rearrange("p t (s e) -> p t s e", e=DH)
            x1, x2 = xs[:, :, :, 0:8], xs[:, :, :, 8:16]
            cb = cosb.unsqueeze(2).to_broadcast([P, NT, 2 * NH, 8])
            sn = sinb.unsqueeze(2).to_broadcast([P, NT, 2 * NH, 8])
            nc.vector.tensor_tensor(rot[0], x1, cb, ALU.mult)
            nc.vector.tensor_tensor(rot[1], x2, sn, ALU.mult)
            nc.vector.tensor_tensor(rot[2], x2, cb, ALU.mult)
            link(dve, nc.vector.tensor_tensor(rot[3], x1, sn, ALU.mult))
            nc.vector.tensor_tensor(x1, rot[0], rot[1], ALU.subtract)
            nc.vector.tensor_tensor(x2, rot[2], rot[3], ALU.add).then_inc(rope_done, 1)

        def tile_of(t, n):
            return t[:, :, n * P:(n + 1) * P]

        A, E, O = (lambda f: (UNITS["A%d" % f], D)), (UNITS["EG"], D), (UNITS["OT"], BW)

        @block.scalar
        def _(act):
            act.dma_start(con[:, :], a["consts"]).then_inc(con_in, 16)
            act.wait_ge(par_in, 16 * 9)
            act.wait_ge(lam_sum, 1)
            nc.scalar.activation(lamc[:, 2:4], lamc[:, 0:2], ACT.Exp).then_inc(lam_exp, 1)
            nc.scalar.activation(wf_hi[:, :, :], wf_raw, ACT.Copy).then_inc(wf_hi_done, 1)
            act_norm(act, -1, A(0))
            act_ffn(act, 0, 0)
            act_norm(act, 0, E)
            act_even_pairs(act)
            act_blocks(act, "ET", [lambda t: tok[:, t, LW:D], lambda t: tok[:, t, 0:LW], lambda t: vE[:, t, :]],
                       0, [1.0, DH ** -0.5, 1.0], lambda b: None)
            act.wait_ge(e_abs, 1)
            nc.scalar.activation(lst2, lst1, ACT.Exp, scale=-1.0).then_inc(e_exp, 1)
            for c in range(CL):
                act_lru(act, c)
            act_sample(act, 0)
            act.wait_ge(hl_ps, 1)
            nc.scalar.activation(hl_rows[0:64, :], ps[0:64, 7, :], ACT.Copy).then_inc(hl_copied, 1)
            act_prompt(act, 0)
            for t in range(NT):
                act_xt(act, "yE", t, t, CL)
            act_mix_out(act, "EO", 1)
            act_norm(act, 1, A(1))
            act_ffn(act, 1, 2)
            act_norm(act, 2, A(2))
            act_ffn(act, 2, 3)
            act_norm(act, 3, O)

            def before(b):
                if b == 4:
                    act.wait_ge(tr_mm, 20)
                    act.wait_ge(k_out, 64)
            act_blocks(act, "OT", [lambda t: tok[:, t, 0:BW], lambda t: tok[:, t, BW:D],
                                   lambda t: vO[:, t, 0:BW], lambda t: vO[:, t, BW:D],
                                   lambda t: tok[:, t, 0:BW], lambda t: tok[:, t, BW:D]],
                       15, [1.0] * 4 + [DH ** -0.5] * 2, before)
            act_sample(act, 1)
            act_prompt(act, 1)
            for j in range(NT):
                act_xt(act, "yO", j, (j + NP) % NT)
            act_mix_out(act, "OO", 4)
            act_norm(act, 4, A(3))
            act_ffn(act, 3, 5)
            act_norm(act, 5)

        @block.vector
        def _(dve):
            dve.wait_ge(par_in, 16 * 9)
            link(dve, nc.vector.tensor_tensor(lam_pr, lam_in[:, 0:4:2, :], lam_in[:, 1:4:2, :], ALU.mult))
            nc.vector.tensor_reduce(lamc[:, 0:2], lam_pr, AX.X, ALU.add).then_inc(lam_sum, 1)
            dve.wait_ge(lam_exp, 1)
            link(dve, nc.vector.tensor_tensor(lamc[:, 0:1], lamc[:, 2:3], lamc[:, 3:4], ALU.subtract))
            link(dve, nc.vector.tensor_scalar(lamc[:, 0:1], lamc[:, 0:1], LAM_INIT, None, ALU.add))
            nc.vector.tensor_scalar(lamc[:, 1:2], lamc[:, 0:1], -1.0, None, ALU.mult)
            dve.wait_ge(wf_hi_done, 1)
            nc.vector.tensor_tensor(wf_lo[:, :, :], wf_raw, wf_hi[:, :, :].bitcast(F32), ALU.subtract).then_inc(wf_lo_done, 1)
            dve.wait_ge(par_ps, 1)
            nc.vector.tensor_copy(par[:, :, :], bank(7, CL * R_ALL).rearrange("p (c r) -> p c r", r=R_ALL)).then_inc(par_done, 1)
            dve_norm(dve, -1, A(0))
            dve_ffn(dve, 0)
            dve_norm(dve, 0, E)
            dve_even_pairs(dve)
            dve_units(dve, UNITS["ET"] + 2, 3 * KD - 2)
            link(dve, nc.vector.memset(hl, 0.0))
            dve_forget(dve)
            for t in range(NT):
                dve_tr(dve, t, tile_of(kTE, t))
            for t in range(NT):
                dve_tr(dve, NT + t, tile_of(qTE, t))
            for c in range(CL):
                dve_lru(dve, c)
            dve_sample(dve, 0)
            dve_prompt(dve, 0)
            for t in range(NT):
                dve_xt(dve, "yE", t, t, CL)
            dve_units(dve, UNITS["EO"], 2 * KD)
            dve_norm(dve, 1, A(1))
            dve_ffn(dve, 1)
            dve_norm(dve, 2, A(2))
            dve_ffn(dve, 2)
            dve_norm(dve, 3, O)
            u = UNITS["OT"]
            dve_units(dve, u + 2, 2 * KD)
            dve.wait_ge(t_out, 15 + 10)
            rope(dve, 0)
            dve_units(dve, u + 2 + 2 * KD, KD)
            for t in range(NT):
                for j in range(2):
                    dve_tr(dve, 10 + 2 * t + j, tile_of(kTO, t)[:, 4 * j:4 * j + 4, :])
            dve_units(dve, u + 2 + 3 * KD, 3 * KD - 2)
            dve.wait_ge(t_out, 15 + 30)
            rope(dve, 1)
            for t in range(NT):
                for j in range(2):
                    dve_tr(dve, 20 + 2 * t + j, tile_of(qTO, t)[:, 4 * j:4 * j + 4, :])
            dve_sample(dve, 1)
            dve_prompt(dve, 1)
            for j in range(NT):
                dve_xt(dve, "yO", j, (j + NP) % NT)
            dve_units(dve, UNITS["OO"], 2 * KD)
            dve_norm(dve, 4, A(3))
            dve_ffn(dve, 3)
            dve_norm(dve, 5)

        @block.tensor
        def _(pe):
            pe.wait_ge(con_in, 16)
            pe.wait_ge(par_in, 16 * 9)
            for c in range(CL):
                mm = nc.tensor.transpose(bank(7, R_ALL, c * R_ALL), prow[0:R_ALL, c * P:(c + 1) * P],
                                         con[0:R_ALL, C_ID:C_ID + R_ALL])
            mm.then_inc(par_ps, 1)

            def norm(p):
                for t in range(NT):
                    pe_xt(pe, "pre%d" % p, t, t)
            norm(0)
            pe.wait_ge(par_done, 1)
            pe_pairs(pe, "A0", XT["pre0"], KF)
            pe_ffn_out(pe, 0, 0)
            norm(1)
            pe_pairs(pe, "EG", XT["pre1"], CL)
            pe_blocks(pe, "ET", 0, 3, 0,
                      lambda t: pe.wait_ge(h_done, 2 * (CHUNKS["EG"] + CL) - (0 if t == 4 else 2)))
            pe_forget(pe)
            pe_cumulate(pe)
            pe.wait_ge(t_out, 5)
            for t in range(NT):
                pe_tr(pe, t, tok[:, t, LW:D])
            pe.wait_ge(t_out, 10)
            for t in range(NT):
                pe_tr(pe, NT + t, tok[:, t, 0:LW])
            for c in range(CL):
                pe_gates(pe, c)
            pe_sample(pe, 0)
            pe_last_rows(pe)
            pe_prompt(pe, 0)
            pe.wait_ge(o_done, NSTEP)
            for t in range(NT):
                pe_xt(pe, "yE", t, t, CL)
            pe_mix_out(pe, "EO", 1, "yE")
            norm(2)
            pe_pairs(pe, "A1", XT["pre2"], KF)
            pe_ffn_out(pe, 1, 2)
            norm(3)
            pe_pairs(pe, "A2", XT["pre3"], KF)
            pe_ffn_out(pe, 2, 3)
            norm(4)
            pe_blocks(pe, "OT", 0, 3, 15, lambda t: pe.wait_ge(xt_lo, XT["pre4"] + NT))
            pe.wait_ge(rope_done, 1)
            for t in range(NT):
                for j in range(2):
                    pe_tr(pe, 10 + 2 * t + j, tok[:, t, j * BW:(j + 1) * BW])
            pe_blocks(pe, "OT", 3, 3, 30)
            pe.wait_ge(rope_done, 2)
            for t in range(NT):
                for j in range(2):
                    pe_tr(pe, 20 + 2 * t + j, tok[:, t, j * BW:(j + 1) * BW])
            pe_sample(pe, 1)
            pe_prompt(pe, 1)
            for j in range(NT):
                pe_xt(pe, "yO", j, (j + NP) % NT)
            pe_mix_out(pe, "OO", 4, "yO")
            norm(5)
            pe_pairs(pe, "A3", XT["pre5"], KF)
            pe_ffn_out(pe, 3, 5)

        @block.gpsimd
        def _(pool):
            rows = [(R_BUF, 24, a["state_lru_conv"][0].rearrange("s j c -> (s j) c")),
                    (R_H0, NS, a["state_lru_h"][0]), (R_CW, CW, a["lru_conv_w"][0]),
                    (R_CB, 1, a["lru_conv_b"]), (R_LAM, 1, a["lru_lambda"])]
            for r, n, src in rows:
                pool.dma_start(prow[r:r + n, :], src).then_inc(par_in, 16)
            pool.dma_start(prow[R_BR:R_BI + 1, :].rearrange("j (n g) -> j n g", g=DH),
                           a["lru_b_gates"][0].rearrange("n (j g) -> j n g", g=DH)).then_inc(par_in, 16)
            pool.dma_start(wf_raw, a["w_in_even"][0].rearrange("(k p) n -> p k n", p=P)[:, :, 2 * LW + 3 * LW:])\
                .then_inc(par_in, 16)
            pool.dma_start(bfb, a["b_fox_f"][0].partition_broadcast(P)).then_inc(par_in, 16)
            pool.dma_start(lam_in.rearrange("p a b -> p (a b)"), a["diff_lambda"][0].rearrange("a b -> (a b)")
                           .partition_broadcast(P)).then_inc(par_in, 16)
            pool_gain_pre(pool, 0)
            pool_gain_post(pool, 0)
            nc.gpsimd.memset(nhalf, -0.5).then_inc(gs, 1)
            pool_count[0] += 1
            pool.wait_ge(gs, pool_count[0])
            pool_norm(pool, -1)
            pool_gain_pre(pool, 1)
            pool_norm(pool, 0)
            pool_gain_post(pool, 1)
            pool_gain_pre(pool, 2)
            pool.wait_ge(lo_done, UNITS["EG"])
            nc.gpsimd.memset(w_gate, 0.0).then_inc(gs, 1)
            pool_count[0] += 1
            pool.wait_ge(gs, pool_count[0])
            for e in range(2):
                for j in range(2):
                    pool.dma_start(w_gate[64 * e:64 * e + 64, :, j, 64 * e:64 * e + 64],
                                   a["lru_w_gates"][0, e:8:2, :, 64 * j:64 * j + 64].rearrange("c k g -> k c g"))\
                        .then_inc(wg_in, 16)
            pool.dma_start(lfp, a["cache_fox_logf"][0].rearrange("s t h -> t s h")).then_inc(lf_in, 16)

            def store(name, tile, done):
                pool.dma_start(o["p_" + name][0, 0].rearrange("(t p) h d -> p t (h d)", p=P), tile[:, 0:NP, :])\
                    .then_inc(done, 16)
                pool.dma_start(o["s_" + name][0].rearrange("s t h d -> (s t) (h d)"), tile[:, NP, :]).then_inc(done, 16)

            pool.wait_ge(t_out, 5)
            store("fox_k", tok[:, :, LW:D], k_out)
            pool.wait_ge(t_out, 15)
            store("fox_v", vE, v_out)
            pool.wait_ge(logf_done, 1)
            pool.dma_start(o["p_fox_logf"][0, 0].rearrange("(t p) h -> p t h", p=P), lgf[:, 0:NP, :]).then_inc(out_sem2, 16)
            pool.dma_start(o["s_fox_logf"][0].rearrange("s t h -> (s t) h"), lgf[:, NP, :]).then_inc(out_sem2, 16)
            pool.wait_ge(hl_copied, 1)
            for name, r, n, form in [("p_lru_h", 0, 1, None), ("s_lru_h", 1, NS, None),
                                     ("p_lru_conv", 9, 3, "s j c -> (s j) c"), ("s_lru_conv", 12, 24, "s j c -> (s j) c")]:
                dst = o[name][0]
                pool.dma_start(dst.rearrange(form) if form else dst, hl_rows[r:r + n, :]).then_inc(out_sem2, 16)
            pool.wait_ge(out_sem2, 16 * 6)
            pool_norm(pool, 1)
            pool_gain_post(pool, 2)
            pool_gain_pre(pool, 3)
            pool_norm(pool, 2)
            pool_gain_post(pool, 3)
            pool_gain_pre(pool, 4)
            pool_norm(pool, 3)
            pool.wait_ge(x_done, 5 * 4)
            pool.dma_start(sub_g, a["diff_subln_g"][0].partition_broadcast(P)).then_inc(subg_in, 16)
            pool.wait_ge(rope_done, 1)
            store("diff_k", tok, k_out)
            pool.wait_ge(t_out, 15 + 20)
            store("diff_v", vO, v_out)
            for k in range(NT):
                pool.wait_ge(sq_done, k + 1)
                nc.gpsimd.tensor_scalar(s_ss, s_ss, 1.0 / P, EPS, ALU.mult, ALU.add).then_inc(gs, 1)
                pool_count[0] += 1
                pool.wait_ge(gs, pool_count[0])
                nc.gpsimd.tensor_tensor(s_rs, s_ss, nhalf.to_broadcast([P, NH]), ALU.pow).then_inc(srs_done, 1)
            pool_gain_post(pool, 4)
            pool_gain_pre(pool, 5)
            pool_norm(pool, 4)
            pool_gain_post(pool, 5)
            pool_norm(pool, 5)


_INS = ['x_prompt', 'x_sample', 'cache_fox_k', 'cache_fox_v', 'cache_fox_logf', 'state_lru_h', 'state_lru_conv',
        'cache_diff_k', 'cache_diff_v', 'norm_g', 'w_ffn_in', 'w_ffn_out', 'w_in_even', 'b_fox_f', 'lru_conv_w',
        'lru_conv_b', 'lru_w_gates', 'lru_b_gates', 'lru_lambda', 'w_out_even', 'w_in_odd', 'diff_lambda',
        'diff_subln_g', 'w_out_odd']


def _group(prefix, b, t):
    return [(prefix + 'fox_k', (1, b, t, NH, DH)), (prefix + 'fox_v', (1, b, t, NH, DH)),
            (prefix + 'fox_logf', (1, b, t, NH)), (prefix + 'lru_h', (1, b, LW)),
            (prefix + 'lru_conv', (1, b, CW - 1, LW)), (prefix + 'diff_k', (1, b, t, NH, P)),
            (prefix + 'diff_v', (1, b, t, NH, P))]


_OUTS = [('y_prompt', (1, SEQ, D)), ('y_sample', (NS, TS, D))] + _group('p_', 1, SEQ) + _group('s_', NS, TS)


def _constants():
    import numpy as np
    i, j = np.arange(P)[:, None], np.arange(P)[None, :]
    c = np.zeros((P, C_ALL), np.float32)
    c[:, C_ID:C_ID + P] = i == j
    c[:, C_UT:C_UT + P] = i <= j
    c[:, C_ONE:C_ONE + 3 * P] = 1
    c[:, C_SL:C_SL + P] = i > j
    c[:, C_NT:C_NT + P] = np.where(j > i, NEG, 0)
    c[:, C_NC:C_NC + P] = np.where(j // CHUNK > i // CHUNK, NEG, 0)
    c[:, C_UB:C_UB + P] = (i // TS == j // TS) & (i <= j)
    pos = np.concatenate([np.arange(SEQ), PAST + np.tile(np.arange(TS), NS)]).astype(np.float32).reshape(NT, P).T
    inv = (np.float32(500000.0) ** (-np.arange(8, dtype=np.float32) * np.float32(2.0 / 16))).astype(np.float32)
    ang = (pos[:, :, None] * inv).astype(np.float32)
    c[:, C_COS:C_COS + NT * 8] = np.cos(ang).reshape(P, -1)
    c[:, C_SIN:C_SIN + NT * 8] = np.sin(ang).reshape(P, -1)
    c[:, C_NS:C_NS + TS] = np.where(np.arange(TS)[None, :] > i % TS, NEG, 0)
    return c


def kernel(**inputs):
    import numpy as _np
    import concourse.bacc as _bacc
    from concourse.bass_utils import run_bass_kernel_spmd as _run

    nc = _bacc.Bacc("TRN2", target_bir_lowering=False, num_devices=1)
    arrays, ins, outs = {}, {}, {}
    for name, v in [(n, inputs[n]) for n in _INS] + [("consts", _constants())]:
        v = _np.ascontiguousarray(v)
        arrays["in_" + name] = v
        ins[name] = nc.dram_tensor("in_" + name, v.shape, F32, kind="ExternalInput").ap()
    for name, shape in _OUTS:
        outs[name] = nc.dram_tensor("out_" + name, shape, F32, kind="ExternalOutput").ap()
    build_trunk(nc, ins, outs)
    r = _run(nc, [arrays], core_ids=[0])
    return tuple(r.results[0]["out_" + name] for name, _ in _OUTS)
```

```python
from contextlib import ExitStack

import concourse.bass as bass
from concourse import mybir

F32 = mybir.dt.float32
F32R = mybir.dt.float32r
ACT = mybir.ActivationFunctionType
ALU = mybir.AluOpType
AX = mybir.AxisListType

P = 128
EPS = 1e-6
D = 1024
KD = D // P
SEQ = 512
NS, TS = 8, 16
PAST = 128
TOK = SEQ + NS * TS
NT = TOK // P
NP = SEQ // P
FF = 2816
KF = FF // P
HALVES = [(0, 256), (256, 384)]
LW = 512
CL = LW // P
NH = 8
DH = 64
CW = 4
UP = CW - 1 + SEQ
US = CW - 1 + TS
UW = UP + NS * US
CHUNK = 64
NEG = -1e30
LAM_INIT = 0.8 - 0.6 * 2.718281828459045 ** -0.3
BW = 512
SLOT = BW + TOK

C_ID, C_UT, C_ONE, C_SL, C_NT, C_NC, C_UB = (i * P for i in (0, 1, 2, 5, 6, 7, 8))
C_COS = 9 * P
C_SIN = C_COS + NT * 8
C_NS = C_SIN + NT * 8
C_ALL = C_NS + TS

R_BUF, R_H0, R_CW, R_CB, R_LAM, R_BR, R_BI = 0, 24, 32, 36, 37, 38, 39
R_ALL = 40

UNITS = {}
_at = 0
for _name, _n in [("A0", 2 * KF), ("B0", 2 * KF), ("EG", 2 * CL), ("ET", 3 * KD), ("EO", 2 * KD),
                  ("A1", 2 * KF), ("B1", 2 * KF), ("A2", 2 * KF), ("B2", 2 * KF),
                  ("OT", 6 * KD), ("OO", 2 * KD), ("A3", 2 * KF), ("B3", 2 * KF)]:
    UNITS[_name] = _at
    _at += _n
RESULT = [(UNITS[_n], KD if _n[1] == "O" else KF) for _n in ("B0", "EO", "B1", "B2", "OO", "B3")]
CHUNKS = {"A0": 0, "EG": KF, "A1": KF + CL, "A2": 2 * KF + CL, "A3": 3 * KF + CL}
XT = {"pre0": 0, "pre1": 5, "yE": 10, "pre2": 15, "pre3": 20, "pre4": 25, "yO": 30, "pre5": 35}
READY = {"pre0": 0, "pre1": 5, "pre2": 10, "pre3": 15, "pre4": 20, "yO": 25, "pre5": 30}
GAIN_PRE = [(0, 0), (0, 2), (0, 4), (1, 0), (1, 2), (1, 4)]
GAIN_POST = [(0, 1), (0, 3), (0, 5), (1, 1), (1, 3), (1, 5)]
STEP = [0.5, 1.0, 0.5, 0.5, 1.0, 0.5]


def build_trunk(nc, a, o):
    ctx = ExitStack()
    with ctx:
        def sb(name, shape, dt=F32):
            return ctx.enter_context(nc.sbuf_tensor(name, shape, dt))

        def sem(name):
            return ctx.enter_context(nc.semaphore(name))

        x = sb("x", [P, NT, D])
        tok = sb("tok", [P, NT, D])
        xT_hi = sb("xT_hi", [P, KD, TOK], F32R)
        xT_lo = sb("xT_lo", [P, KD, TOK], F32R)
        raw = sb("raw", [P, 4, D])
        w_hi = sb("w_hi", [P, 2, SLOT], F32R)
        w_lo = sb("w_lo", [P, 2, SLOT], F32R)
        gain = sb("gain", [P, 2, D])
        arena = sb("arena", [P, 3 * NT * D])
        att = sb("att", [P, 3456])
        scratch = sb("scratch", [P, D])
        con = sb("con", [P, C_ALL])
        par = sb("par", [P, CL, R_ALL])
        small = sb("small", [P, 512])
        ps = ctx.enter_context(nc.psum_tensor("ps", [P, 8, 512], F32))
        psf = ps[:, :, :].rearrange("p b n -> p (b n)")

        def view(t, at, *dims):
            n = 1
            for d in dims:
                n *= d
            flat = t[:, at:at + n]
            if len(dims) == 1:
                return flat
            names = "abcd"[:len(dims)]
            return flat.rearrange("p (%s) -> p %s" % (" ".join(names), " ".join(names)),
                                  **{k: d for k, d in zip(names[1:], dims[1:])})

        hid = view(arena, 0, KF, TOK)
        silu = view(scratch, 0, 2, 384)
        ss_m, ss_x, rs_m, rs_x, vtmp = (view(small, 8 * i, 8) for i in range(5))
        nhalf = small[:, 40:41]
        lgf = view(small, 48, NT, NH)
        ls_all = small[:, 48:92]
        cl_a, cl_t = small[:, 92:96], small[:, 96:100]
        rneg, rsum, rinv = (view(small, 100 + 8 * i, 2, 4) for i in range(3))
        lamc = small[:, 132:136]
        bfb = small[:, 136:144]
        lsz, lst1, lst2, lst3 = (small[:, 144 + 44 * i:188 + 44 * i] for i in range(4))
        cq = view(small, 480, NP, NH)
        h0a = small[:, 320:328]
        s_ss = small[:, 464:472]
        s_rs = small[:, 472:480]
        ident = con[:, C_ID:C_ID + P]
        ones = con[:, C_ONE:C_ONE + P]

        raw_in = [sem("raw_in%d" % j) for j in range(4)]
        hi_done = sem("hi_done")
        lo_done = sem("lo_done")
        used = sem("used")
        a_mm = sem("a_mm")
        silu_done = sem("silu_done")
        h_done = sem("h_done")
        m_mm = sem("m_mm")
        m_out = sem("m_out")
        x_in = [sem("x_in%d" % t) for t in range(NT)]
        con_in, par_in = sem("con_in"), sem("par_in")
        gpost_in, gpre_in = sem("gpost_in"), sem("gpre_in")
        ss_m_done, ss_x_done = sem("ss_m_done"), sem("ss_x_done")
        rs_m_done, rs_x_done = sem("rs_m_done"), sem("rs_x_done")
        x_done = sem("x_done")
        tok_ready = sem("tok_ready")
        xt_ps = sem("xt_ps")
        xt_hi, xt_lo = sem("xt_hi"), sem("xt_lo")
        vs, ss_, gs = sem("vector_step"), sem("scalar_step"), sem("pool_step")
        t_mm, t_out = sem("t_mm"), sem("t_out")
        tr_mm, tr_out = sem("tr_mm"), sem("tr_out")
        rope_done, pairs_done = sem("rope_done"), sem("pairs_done")
        k_out, v_out = sem("k_out"), sem("v_out")
        f_mm, f_out, ft_mm = sem("f_mm"), sem("f_out"), sem("ft_mm")
        logf_done = sem("logf_done")
        par_ps, par_done = sem("par_ps"), sem("par_done")
        wg_in = sem("wg_in")
        wf_hi_done, wf_lo_done = sem("wf_hi_done"), sem("wf_lo_done")
        e_abs, e_exp = sem("e_abs"), sem("e_exp")
        cq_mm, cq_done = sem("cq_mm"), sem("cq_done")
        conv_done, gate_mm = sem("conv_done"), sem("gate_mm")
        r_done, i_done, a_done, t_done = sem("r_done"), sem("i_done"), sem("a_done"), sem("t_done")
        m2_done, m_done = sem("m2_done"), sem("m_done")
        gz_done, gs_done, ya_done, ya_hi = sem("gz_done"), sem("gs_done"), sem("ya_done"), sem("ya_hi")
        hl_ready, hl_ps, hl_copied = sem("hl_ready"), sem("hl_ps"), sem("hl_copied")
        lru_end = sem("lru_end")
        out_sem = sem("y_stored")
        out_sem2 = sem("states_stored")
        subg_in, subg_done = sem("subg_in"), sem("subg_done")
        kc_in = [sem("kc_in0"), sem("kc_in1")]
        vc_in = [sem("vc_in0"), sem("vc_in1")]
        lf_in = sem("lf_in")
        kt_mm, kt_done = sem("kt_mm"), sem("kt_done")
        qb_done, ssc_mm, smax_done, sp_done = sem("qb_done"), sem("ssc_mm"), sem("smax_done"), sem("sp_done")
        sa_done, sat_mm, sat_done = sem("sa_done"), sem("sat_mm"), sem("sat_done")
        so_mm, so_done, sot_mm, sot_done = sem("so_mm"), sem("so_done"), sem("sot_mm"), sem("sot_done")
        pn_mm, pn_done, sn_mm, sn_done = sem("pn_mm"), sem("pn_done"), sem("sn_mm"), sem("sn_done")
        lam_exp, lam_sum = sem("lam_exp"), sem("lam_sum")
        nc_mm, nc_done = sem("nc_mm"), sem("nc_done")
        qk_mm, s_read, s_ready, p_done, c_done = sem("qk_mm"), sem("s_read"), sem("s_ready"), sem("p_done"), sem("c_done")
        pt_mm, pt_done, pv_mm, o_done = sem("pt_mm"), sem("pt_done"), sem("pv_mm"), sem("o_done")
        sq_done, srs_done = sem("sq_done"), sem("srs_done")

        block = ctx.enter_context(nc.Block())

        u_pad = view(arena, 0, CL, UW)
        gate = view(arena, CL * UW, CL, TOK)
        at = CL * UW + CL * TOK
        vE = view(arena, at, NT, LW)
        qTE = view(arena, at + NT * LW, CL, TOK)
        kTE = view(arena, at + 2 * NT * LW, CL, TOK)
        at += 3 * NT * LW
        w_gate = view(arena, at, CL, 2, P)
        at += 2 * CL * P
        lfp = view(arena, at, NS, NH)
        prod = view(arena, at + 64, P)
        wf = sb("wf", [P, KD, 2 * NH], F32R)
        nlb = view(arena, at + 192, P)
        lfp_b = view(arena, at + 320, P)
        lgn = view(arena, at + 448, NT, NH)
        hl_rows = view(arena, at + 488, LW)
        prow = view(att, 0, LW)
        wf_raw = view(att, LW, KD, NH)
        lam_in = view(att, 576, 4, DH)
        lam_pr = view(att, 832, 2, DH)
        conv_u, gelu_g = kTE, qTE
        r_c, i_c, t_c = (view(att, TOK * i, TOK) for i in range(3))
        f_rows = att[0:2 * NH, 3 * TOK:4 * TOK]
        hl = view(scratch, LW, CL, P)
        vO = view(arena, 0, NT, D)
        qTO = view(arena, NT * D, KD, TOK)
        kTO = view(arena, 2 * NT * D, KD, TOK)
        rot = [view(att, 640 * i, NT, 2 * NH, 8) for i in range(4)]
        sub_g = small[:, 124:125]
        negc = view(scratch, 0, 2, 512)
        stE = view(att, 0, 4, 512)
        ptE = view(att, 2048, 2, 4, P)
        pO = view(att, 0, 3, 2, 512)
        ptO = gain[:, 1, :].rearrange("p (a b c) -> p a b c", a=2, b=4)
        kts = [view(att, 1152 * i, KD, PAST + TS) for i in range(2)]
        qbd = view(att, 2304, D + P)
        s_sp = [view(att, 2944, 1, PAST + TS), gain[:, 1, 0:288].rearrange("p (m n) -> p m n", m=2)]
        s_sa = [att[:, 3088:3344], gain[:, 1, 288:544]]
        s_sat = [view(att, 2016, P), gain[:, 1, 544:672]]
        pn_flat = view(att, 0, NH * P)
        ones3 = con[:, C_ONE:C_ONE + 3 * P]
        pn_b = view(att, 0, NH, NS, TS)

        cosb = view(con, C_COS, NT, 8)
        sinb = view(con, C_SIN, NT, 8)

        def bank(b, n=512, at=0):
            return ps[:, b, at:at + n]

        def out_bank(n, t):
            return (5 * n + t) % 8

        def sp_unit(sp, u, it, src):
            if it is not None or u >= 4:
                sp.wait_ge(lo_done, (u - 3) + 4 * it if it is not None else u - 3)
            dst = raw[:, u % 4, 0:src.shape[-1]] if len(src.shape) == 2 else \
                raw[:, u % 4, :].rearrange("p (k n) -> p k n", n=P)
            sp.dma_start(dst, src).then_inc(raw_in[u % 4], 16)

        def sp_pairs(sp, name, w, stride, pairs):
            u0 = UNITS[name]
            wv = w.rearrange("(k p) n -> p k n", p=P)

            def some(c, it):
                for cc in range(2):
                    for which in range(2):
                        u = u0 + 2 * cc + which + 2 * c
                        if it is None:
                            src = wv[:, :, which * stride + (c + cc) * P:which * stride + (c + cc + 1) * P]
                        else:
                            src = wv[:, :, bass.ds(which * stride + cc * P + it * (2 * P), P)]
                        sp_unit(sp, u, it, src)
            some(0, None)
            with sp.Fori(1, pairs // 2, 1) as it:
                some(0, it)

        def sp_rows(sp, u0, w, blocks, rows):
            for b, c0 in enumerate(blocks):
                wb = w[:, c0:c0 + BW].rearrange("(k p) n -> p k n", p=P)
                full = rows // 4
                with sp.Fori(0, full, 1) as it:
                    for j in range(4):
                        u = u0 + b * rows + j
                        src = wb[:, bass.ds(it * 4 + j, 1), :].rearrange("p a n -> p (a n)")
                        sp_unit(sp, u, it, src)
                for k in range(4 * full, rows):
                    sp_unit(sp, u0 + b * rows + k, None, wb[:, k, :])

        def sp_ffn(sp, f):
            l, j = divmod(f, 2)
            sp_pairs(sp, "A%d" % f, a["w_ffn_in"][l, j], FF, KF)
            sp_rows(sp, UNITS["B%d" % f], a["w_ffn_out"][l, j], [0, BW], KF)

        def sp_caches(sp, odd):
            w = (1 + odd) * 512
            kc, vc = (a["cache_diff_k"], a["cache_diff_v"]) if odd else (a["cache_fox_k"], a["cache_fox_v"])

            def keys(s):
                if s >= 2:
                    sp.wait_ge(kt_mm, NS * odd + s - 1)
                if odd:
                    for m in range(2):
                        sp.dma_start(raw[:, s % 2, m * BW:(m + 1) * BW].rearrange("p (h d) -> p h d", d=DH),
                                     kc[0, s][:, :, m * DH:(m + 1) * DH]).then_inc(kc_in[s % 2], 16)
                else:
                    sp.dma_start(raw[:, s % 2, 0:w], kc[0, s].rearrange("t h d -> t (h d)")).then_inc(kc_in[s % 2], 16)

            def values(s):
                if s >= 2:
                    sp.wait_ge(so_mm, NS * odd + s - 1)
                sp.dma_start(raw[:, 2 + s % 2, 0:w], vc[0, s].rearrange("t h d -> t (h d)")).then_inc(vc_in[s % 2], 16)

            sp.wait_ge(lo_done, UNITS["OO"] if odd else UNITS["EO"])
            keys(0)
            keys(1)
            for s in range(NS):
                if s and s + 1 < NS:
                    keys(s + 1)
                values(s)
            sp.wait_ge(so_mm, NS * (odd + 1))

        @block.sync
        def _(sp):
            for t in range(NT):
                src = a["x_prompt"][0, t * P:(t + 1) * P, :] if t < NP else \
                    a["x_sample"].rearrange("s t d -> (s t) d")
                sp.dma_start(x[:, t, :], src).then_inc(x_in[t], 16)
            sp_ffn(sp, 0)
            sp_pairs(sp, "EG", a["w_in_even"][0], LW, CL)
            sp_rows(sp, UNITS["ET"], a["w_in_even"][0], [3 * LW, 2 * LW, 4 * LW], KD)
            sp_caches(sp, 0)
            sp_rows(sp, UNITS["EO"], a["w_out_even"][0], [0, BW], KD)
            sp_ffn(sp, 1)
            sp_ffn(sp, 2)
            sp_rows(sp, UNITS["OT"], a["w_in_odd"][0], [D, D + BW, 2 * D, 0, BW, 2 * D + BW], KD)
            sp_caches(sp, 1)
            sp_rows(sp, UNITS["OO"], a["w_out_odd"][0], [0, BW], KD)
            sp_ffn(sp, 3)
            for t in range(NT):
                sp.wait_ge(x_done, 5 * 5 + t + 1)
                dst = o["y_prompt"][0, t * P:(t + 1) * P, :] if t < NP else \
                    o["y_sample"].rearrange("s t d -> (s t) d")
                sp.dma_start(dst, x[:, t, :]).then_inc(out_sem, 16)
            sp.wait_ge(out_sem, 16 * NT)

        def act_hi(act, u, it, n):
            act.wait_ge(raw_in[u % 4], 16 * (u // 4 + 1) + (0 if it is None else 16 * it))
            if it is not None or u >= 2:
                act.wait_ge(used, u - 1 if it is None else (u - 1) + 4 * it)
            return nc.scalar.activation(w_hi[:, u % 2, 0:n], raw[:, u % 4, 0:n], ACT.Copy)

        def dve_lo(dve, u, it, n):
            dve.wait_ge(hi_done, u + 1 if it is None else (u + 1) + 4 * it)
            return nc.vector.tensor_tensor(w_lo[:, u % 2, 0:n], raw[:, u % 4, 0:n],
                                           w_hi[:, u % 2, 0:n].bitcast(F32), ALU.subtract)

        def at_chunk(k, it):
            return hid[:, k, :] if it is None else \
                hid[:, bass.ds(it * 4 + k, 1), :].rearrange("p a n -> p (a n)")

        def act_hi_b(act, u, it, k):
            act_hi(act, u, it, BW)
            nc.scalar.activation(w_hi[:, u % 2, BW:SLOT], at_chunk(k, it), ACT.Copy).then_inc(hi_done, 1)

        def dve_lo_b(dve, u, it, k):
            dve_lo(dve, u, it, BW)
            nc.vector.tensor_tensor(w_lo[:, u % 2, BW:SLOT], at_chunk(k, it),
                                    w_hi[:, u % 2, BW:SLOT].bitcast(F32), ALU.subtract).then_inc(lo_done, 1)

        def reg(base, it, per):
            return base if it is None else base + it * per

        def half_ready(eng, u0, c0, c, it, which, half):
            if half == 0:
                eng.wait_ge(a_mm, reg(2 * (c0 + c) + which + 1, it, 4))
            else:
                eng.wait_ge(used, reg(u0 + 2 * c + which + 1, it, 4))

        def act_ffn(act, f, tail):
            u0, c0, b0 = UNITS["A%d" % f], CHUNKS["A%d" % f], UNITS["B%d" % f]

            def gate_half(c, it, half):
                w = HALVES[half][1]
                half_ready(act, u0, c0, c, it, 0, half)
                if it is not None or c0 + c > 0:
                    act.wait_ge(h_done, reg(2 * (c0 + c - 1) + half + 1, it, 4))
                nc.scalar.activation(silu[:, half, 0:w], bank(4 * (c % 2) + half, w), ACT.Silu).then_inc(silu_done, 1)

            def chunk(c, it):
                act_hi(act, u0 + 2 * c + 2, it, D).then_inc(hi_done, 1)
                gate_half(c, it, 0)
                gate_half(c, it, 1)
                act_hi(act, u0 + 2 * c + 3, it, D).then_inc(hi_done, 1)

            chunk(0, None)
            chunk(1, None)
            with act.Fori(1, KF // 2 - 1, 1) as it:
                chunk(0, it)
                chunk(1, it)
            chunk(KF - 2, None)
            c = KF - 1
            act_hi_b(act, b0, None, 0)
            gate_half(c, None, 0)
            gate_half(c, None, 1)
            act.wait_ge(h_done, 2 * (c0 + KF))
            act_hi_b(act, b0 + 1, None, 1)
            for k in range(2, 4):
                act_hi_b(act, b0 + k, None, k)
            with act.Fori(1, KF // 4, 1) as it:
                for k in range(4):
                    act_hi_b(act, b0 + k, it, k)
            for k in range(4 * (KF // 4), KF):
                act_hi_b(act, b0 + k, None, k)
            for k in range(2):
                act_hi_b(act, b0 + KF + k, None, k)
            act_result(act, tail, 0)
            with act.Fori(0, KF // 4, 1) as it:
                for k in range(4):
                    act_hi_b(act, b0 + KF + 2 + k, it, k + 2)

        def dve_ffn(dve, f):
            u0, c0, b0 = UNITS["A%d" % f], CHUNKS["A%d" % f], UNITS["B%d" % f]

            def hidden_half(c, it, half):
                at0, w = HALVES[half]
                half_ready(dve, u0, c0, c, it, 1, half)
                dve.wait_ge(silu_done, reg(2 * (f * KF + c) + half + 1, it, 4))
                dst = hid[:, c, at0:at0 + w] if it is None else \
                    hid[:, bass.ds(it * 2 + c, 1), at0:at0 + w].rearrange("p a n -> p (a n)")
                nc.vector.tensor_tensor(dst, silu[:, half, 0:w], bank(4 * (c % 2) + 2 + half, w),
                                        ALU.mult).then_inc(h_done, 1)

            def chunk(c, it):
                dve_lo(dve, u0 + 2 * c + 2, it, D).then_inc(lo_done, 1)
                hidden_half(c, it, 0)
                hidden_half(c, it, 1)
                dve_lo(dve, u0 + 2 * c + 3, it, D).then_inc(lo_done, 1)

            chunk(0, None)
            chunk(1, None)
            with dve.Fori(1, KF // 2 - 1, 1) as it:
                chunk(0, it)
                chunk(1, it)
            chunk(KF - 2, None)
            c = KF - 1
            dve_lo_b(dve, b0, None, 0)
            hidden_half(c, None, 0)
            hidden_half(c, None, 1)
            dve.wait_ge(h_done, 2 * (c0 + KF))
            for k in range(1, 4):
                dve_lo_b(dve, b0 + k, None, k)
            with dve.Fori(1, KF // 4, 1) as it:
                for k in range(4):
                    dve_lo_b(dve, b0 + k, it, k)
            for k in range(4 * (KF // 4), KF):
                dve_lo_b(dve, b0 + k, None, k)
            for k in range(2):
                dve_lo_b(dve, b0 + KF + k, None, k)
            with dve.Fori(0, KF // 4, 1) as it:
                for k in range(4):
                    dve_lo_b(dve, b0 + KF + 2 + k, it, k + 2)

        def pe_norm(pe, p, tiles=range(NT)):
            for t in tiles:
                if t == 1 and p:
                    pe.wait_ge(m_out, 10 * (p - 1) + 8)
                pe_xt(pe, "pre%d" % p, t, t)

        def pe_pairs(pe, name, p, chunks, meanwhile=None):
            u0, c0 = UNITS[name], CHUNKS[name]

            def product(c, it, which, half):
                u = u0 + 2 * c + which
                at0, w = HALVES[half]
                if half == 0:
                    pe.wait_ge(lo_done, reg(u + 1, it, 4))
                if which == 0 and (it is not None or c0 + c >= 2):
                    pe.wait_ge(h_done, reg(2 * (c0 + c - 2) + half + 1, it, 4))
                dst = bank(4 * (c % 2) + 2 * which + half, w)
                for k in range(KD):
                    wh = w_hi[:, u % 2, k * P:(k + 1) * P]
                    wl = w_lo[:, u % 2, k * P:(k + 1) * P]
                    xh, xl = xT_hi[:, k, at0:at0 + w], xT_lo[:, k, at0:at0 + w]
                    nc.tensor.matmul(dst, wl, xh, start=(k == 0), stop=False)
                    nc.tensor.matmul(dst, wh, xl, start=False, stop=False)
                    mm = nc.tensor.matmul(dst, wh, xh, start=False, stop=(k == KD - 1))
                mm.then_inc((a_mm, used)[half], 1)

            def chunk(c, it):
                for which in range(2):
                    for half in range(2):
                        product(c, it, which, half)

            pe_norm(pe, p, range(0, 3))
            pe.wait_ge(xt_lo, XT["pre%d" % p] + 2)
            product(0, None, 0, 0)
            pe_norm(pe, p, range(3, 5))
            product(0, None, 1, 0)
            pe.wait_ge(xt_lo, XT["pre%d" % p] + NT)
            if meanwhile:
                meanwhile()
            product(0, None, 0, 1)
            product(0, None, 1, 1)
            if meanwhile:
                pe.wait_ge(par_done, 1)
            chunk(1, None)
            with pe.Fori(1, chunks // 2, 1) as it:
                chunk(0, it)
                chunk(1, it)

        def pe_row_unit(pe, u, it, k, lhs, banks, start, stop, before=None, done=None):
            pe.wait_ge(lo_done, reg(u + 1, it, 2))
            wh, wl = w_hi[:, u % 2, 0:BW], w_lo[:, u % 2, 0:BW]
            for t in range(NT):
                if before:
                    before(t)
                xh, xl = lhs(u, k, t)
                dst = bank(banks[t])
                nc.tensor.matmul(dst, xl, wh, start=start, stop=False)
                nc.tensor.matmul(dst, xh, wl, start=False, stop=False)
                mm = nc.tensor.matmul(dst, xh, wh, start=False, stop=stop)
                if done is not None and t < NT - 1:
                    mm.then_inc(done, 1)
            mm.then_inc(used, 1)

        def pe_last_units(pe, u, k, lhs, banks):
            pe.wait_ge(lo_done, u + 2)
            for t in range(NT):
                dst = bank(banks[t])
                for j in range(2):
                    wh, wl = w_hi[:, (u + j) % 2, 0:BW], w_lo[:, (u + j) % 2, 0:BW]
                    xh, xl = lhs(u + j, k + j, t)
                    nc.tensor.matmul(dst, xl, wh, start=False, stop=False)
                    nc.tensor.matmul(dst, xh, wl, start=False, stop=False)
                    mm = nc.tensor.matmul(dst, xh, wh, start=False, stop=(j == 1))
                    if t == NT - 1:
                        mm.then_inc(used, 1)
                    elif j == 1:
                        mm.then_inc(m_mm, 1)

        def slot_lhs(u, k, t):
            at0 = BW + t * P
            return w_hi[:, u % 2, at0:at0 + P], w_lo[:, u % 2, at0:at0 + P]

        def xt_lhs(u, k, t):
            return xT_hi[:, k, t * P:(t + 1) * P], xT_lo[:, k, t * P:(t + 1) * P]

        def pe_ffn_out(pe, f, p):
            b0, c_end = UNITS["B%d" % f], CHUNKS["A%d" % f] + KF
            for n in range(2):
                banks = [out_bank(n, t) for t in range(NT)]
                u = b0 + n * KF

                def free(t):
                    if n == 0 and t in (0, 4):
                        pe.wait_ge(h_done, 2 * c_end - (2 if t == 0 else 0))
                    if n == 1 and banks[t] < 5:
                        pe.wait_ge(m_out, 10 * p + banks[t] + 1)

                pe_row_unit(pe, u, None, 0, slot_lhs, banks, True, False, before=free)
                pe_row_unit(pe, u + 1, None, 1, slot_lhs, banks, False, False)
                with pe.Fori(1, KF // 2 - 1, 1) as it:
                    pe_row_unit(pe, u, it, 0, slot_lhs, banks, False, False)
                    pe_row_unit(pe, u + 1, it, 1, slot_lhs, banks, False, False)
                if n == 0:
                    pe_row_unit(pe, u + KF - 2, None, 0, slot_lhs, banks, False, False)
                    pe_row_unit(pe, u + KF - 1, None, 1, slot_lhs, banks, False, True, done=m_mm)
                else:
                    pe_last_units(pe, u + KF - 2, 0, slot_lhs, banks)

        def act_result(act, p, n, tiles=range(NT)):
            for t in tiles:
                if t < NT - 1:
                    act.wait_ge(m_mm, 4 * (2 * p + n) + t + 1)
                else:
                    act.wait_ge(used, RESULT[p][0] + RESULT[p][1] * (n + 1))
                nc.scalar.activation(tok[:, t, n * BW:(n + 1) * BW], bank(out_bank(n, t)), ACT.Copy).then_inc(m_out, 1)

        last_square = []

        def act_norm(act, p, nxt=None):
            def square_after(done, count):
                if last_square:
                    act.wait_ge(*last_square.pop())
                last_square.append((done, count))

            def sq_m(t):
                act_result(act, p, 1, [t])
                act.wait_ge(m_out, 10 * p + 5 + t + 1)
                square_after(ss_m_done, 5 * p + t + 1)
                nc.scalar.activation(scratch[:, :], tok[:, t, :], ACT.Square,
                                     accum_out=ss_m[:, t:t + 1]).then_inc(ss_m_done, 1)

            def sq_x(t):
                if p >= 0:
                    act.wait_ge(x_done, 5 * p + t + 1)
                else:
                    act.wait_ge(x_in[t], 16)
                square_after(ss_x_done, 5 * (p + 1) + t + 1)
                nc.scalar.activation(scratch[:, :], x[:, t, :], ACT.Square,
                                     accum_out=ss_x[:, t:t + 1]).then_inc(ss_x_done, 1)

            for t in range(NT + 2):
                if t < NT and p >= 0:
                    sq_m(t)
                if p < 5:
                    if 1 <= t <= NT:
                        sq_x(t - 1)
                    if t >= 2:
                        act_xt(act, "pre%d" % (p + 1), t - 2, t - 2)
                if t == 3 and nxt:
                    for u in range(nxt[0], nxt[0] + 2):
                        act_hi(act, u, None, nxt[1]).then_inc(hi_done, 1)

        def pool_norm(pool, p):
            def inv(t, src, dst, ready, count, done):
                pool.wait_ge(ready, count)
                nc.gpsimd.tensor_scalar(vtmp[:, t:t + 1], src[:, t:t + 1], 1.0 / D, EPS, ALU.mult, ALU.add).then_inc(gs, 1)
                pool_count[0] += 1
                pool.wait_ge(gs, pool_count[0])
                nc.gpsimd.tensor_tensor(dst[:, t:t + 1], vtmp[:, t:t + 1], nhalf, ALU.pow).then_inc(done, 1)

            for t in range(NT + 1):
                if t < NT and p >= 0:
                    inv(t, ss_m, rs_m, ss_m_done, 5 * p + t + 1, rs_m_done)
                if t >= 1 and p < 5:
                    inv(t - 1, ss_x, rs_x, ss_x_done, 5 * (p + 1) + t, rs_x_done)

        def dve_norm(dve, p, nxt=None):
            def post(t):
                if t == 0:
                    dve.wait_ge(gpost_in, 16 * (p + 1))
                dve.wait_ge(rs_m_done, 5 * p + t + 1)
                link(dve, nc.vector.scalar_tensor_tensor(tok[:, t, :], tok[:, t, :], rs_m[:, t:t + 1], gain[:, 0, :],
                                                         ALU.mult, ALU.mult))
                nc.vector.scalar_tensor_tensor(x[:, t, :], tok[:, t, :], STEP[p], x[:, t, :],
                                               ALU.mult, ALU.add).then_inc(x_done, 1)

            def pre(t):
                if t == 0:
                    dve.wait_ge(gpre_in, 16 * (p + 2))
                dve.wait_ge(rs_x_done, 5 * (p + 1) + t + 1)
                nc.vector.scalar_tensor_tensor(tok[:, t, :], x[:, t, :], rs_x[:, t:t + 1], gain[:, 1, :],
                                               ALU.mult, ALU.mult).then_inc(tok_ready, 1)

            for t in range(NT + 2):
                if t < NT and p >= 0:
                    post(t)
                if p < 5:
                    if 1 <= t <= NT:
                        pre(t - 1)
                    if t >= 2:
                        dve_xt(dve, "pre%d" % (p + 1), t - 2, t - 2)
                if t == 3 and nxt:
                    for u in range(nxt[0], nxt[0] + 2):
                        dve_lo(dve, u, None, nxt[1]).then_inc(lo_done, 1)

        def xt_bank(j):
            return (4 + 2 * (j % 2)) * 512

        def pe_xt(pe, name, j, t, c0=0):
            i = XT[name] + j
            if name in READY:
                pe.wait_ge(tok_ready, READY[name] + j + 1)
            if i >= 2:
                pe.wait_ge(xt_lo, i - 1)
            for c in range(c0, KD):
                mm = nc.tensor.transpose(psf[:, xt_bank(j) + c * P:xt_bank(j) + (c + 1) * P],
                                         tok[:, t, c * P:(c + 1) * P], ident)
            mm.then_inc(xt_ps, 1)

        def xt_src(j, c0):
            return psf[:, xt_bank(j) + c0 * P:xt_bank(j) + D].rearrange("p (c n) -> p c n", n=P)

        def act_xt(act, name, j, t, c0=0):
            i = XT[name] + j
            act.wait_ge(xt_ps, i + 1)
            if name == "yO":
                act.wait_ge(subg_done, 1)
                nc.scalar.activation(xT_hi[:, :, t * P:(t + 1) * P], xt_src(j, 0), ACT.Copy, scale=sub_g).then_inc(xt_hi, 1)
            else:
                nc.scalar.activation(xT_hi[:, c0:KD, t * P:(t + 1) * P], xt_src(j, c0), ACT.Copy).then_inc(xt_hi, 1)

        def dve_xt(dve, name, j, t, c0=0):
            i = XT[name] + j
            dve.wait_ge(xt_hi, i + 1)
            hi = xT_hi[:, c0:KD, t * P:(t + 1) * P].bitcast(F32)
            lo = xT_lo[:, c0:KD, t * P:(t + 1) * P]
            if name == "yO":
                dve.wait_ge(subg_done, 1)
                nc.vector.scalar_tensor_tensor(lo, xt_src(j, 0), sub_g, hi, ALU.mult, ALU.subtract).then_inc(xt_lo, 1)
            else:
                nc.vector.tensor_tensor(lo, xt_src(j, c0), hi, ALU.subtract).then_inc(xt_lo, 1)

        def pool_gain_post(pool, p):
            if p:
                pool.wait_ge(x_done, 5 * p)
            pool.dma_start(gain[:, 0, :], a["norm_g"][GAIN_POST[p][0], GAIN_POST[p][1]].partition_broadcast(P))\
                .then_inc(gpost_in, 16)

        def pool_gain_pre(pool, p):
            if p:
                pool.wait_ge(tok_ready, READY["pre%d" % (p - 1)] + NT)
            if p == 5:
                pool.wait_ge(tok_ready, READY["yO"] + NT)
            pool.dma_start(gain[:, 1, :], a["norm_g"][GAIN_PRE[p][0], GAIN_PRE[p][1]].partition_broadcast(P))\
                .then_inc(gpre_in, 16)

        vcount, scount, pool_count = [0], [0], [0]

        def link(dve, ins):
            vcount[0] += 1
            ins.then_inc(vs, 1)
            dve.wait_ge(vs, vcount[0])

        def slink(act, ins):
            scount[0] += 1
            ins.then_inc(ss_, 1)
            act.wait_ge(ss_, scount[0])

        def pe_blocks(pe, name, first, blocks, t0, start=None, between=None):
            def one(b, it):
                def free(t):
                    if start and it is None and b == 0:
                        start(t)
                    elif t0 or b or it is not None:
                        pe.wait_ge(t_out, reg(t0 + 5 * (b - 1) + t + 1, it, 5))
                for k in range(KD):
                    u = UNITS[name] + (first + b) * KD + k
                    pe.wait_ge(lo_done, reg(u + 1, it, KD))
                    wh, wl = w_hi[:, u % 2, 0:BW], w_lo[:, u % 2, 0:BW]
                    for t in range(NT):
                        if k == 0:
                            free(t)
                        xh, xl = xt_lhs(u, k, t)
                        nc.tensor.matmul(bank(t), xl, wh, start=(k == 0), stop=False)
                        nc.tensor.matmul(bank(t), xh, wl, start=False, stop=False)
                        mm = nc.tensor.matmul(bank(t), xh, wh, start=False, stop=(k == KD - 1))
                        if k == KD - 1 and t < NT - 1:
                            mm.then_inc(t_mm, 1)
                    mm.then_inc(used, 1)
                    if between:
                        between(b * KD + k)
            one(0, None)
            if between:
                for b in range(1, blocks):
                    one(b, None)
            elif blocks > 1:
                with pe.Fori(1, blocks, 1) as it:
                    one(0, it)

        def act_blocks(act, name, dests, t0, scales, before):
            for b in range(len(dests)):
                for k in range(2, KD + (2 if b + 1 < len(dests) else 0)):
                    act_hi(act, UNITS[name] + b * KD + k, None, BW).then_inc(hi_done, 1)
                before(b)
                act_block_out(act, name, b, dests[b], t0, scales[b])

        def act_block_out(act, name, b, dest, t0, scale):
            for t in range(NT):
                if t < NT - 1:
                    act.wait_ge(t_mm, 4 * (t0 // 5 + b) + t + 1)
                else:
                    act.wait_ge(used, UNITS[name] + (b + 1) * KD)
                nc.scalar.activation(dest(t), bank(t), ACT.Copy, scale=scale).then_inc(t_out, 1)

        def dve_units(dve, u0, count):
            with dve.Fori(0, count // 4, 1) as it:
                for j in range(4):
                    dve_lo(dve, u0 + j, it, BW).then_inc(lo_done, 1)
            for j in range(4 * (count // 4), count):
                dve_lo(dve, u0 + j, None, BW).then_inc(lo_done, 1)

        def pe_tr(pe, i, src):
            if i >= 2:
                pe.wait_ge(tr_out, i - 1)
            for c in range(4):
                mm = nc.tensor.transpose(bank(5 + i % 2, P, c * P), src[:, c * P:(c + 1) * P], ident)
            mm.then_inc(tr_mm, 1)

        def pe_tr_odd(pe, i0):
            for t in range(NT):
                if t == NP:
                    pe.wait_ge(pairs_done, i0 // 10)
                for j in range(2):
                    pe_tr(pe, i0 + 2 * t + j, (scratch if t == NP else tok[:, t, :])[:, j * BW:(j + 1) * BW])

        def dve_pairs(dve, k):
            dve.wait_ge(rope_done, k + 1)
            nc.vector.tensor_copy(scratch[:, :].rearrange("p (m h d) -> p m h d", m=2, d=DH),
                                  tok[:, NP, :].rearrange("p (h m d) -> p m h d", m=2, d=DH)).then_inc(pairs_done, 1)

        def dve_tr(dve, i, dst):
            dve.wait_ge(tr_mm, i + 1)
            nc.vector.tensor_copy(dst, bank(5 + i % 2).rearrange("p (c n) -> p c n", n=P)).then_inc(tr_out, 1)

        def pe_mix_out(pe, name, p, y):
            for n in range(2):
                banks = [out_bank(n, t) for t in range(NT)]

                def free(t):
                    if n == 0 and t == 0:
                        pe.wait_ge(xt_lo, XT[y] + NT)
                        if y == "yE":
                            pe.wait_ge(lru_end, CL)
                    if n == 1 and banks[t] < 5:
                        pe.wait_ge(m_out, 10 * p + banks[t] + 1)
                for k in range(KD - 2 * n):
                    u = UNITS[name] + n * KD + k
                    pe_row_unit(pe, u, None, k, xt_lhs, banks, k == 0, k == KD - 1,
                                before=free if k == 0 else None, done=m_mm if k == KD - 1 else None)
            pe_last_units(pe, UNITS[name] + 2 * KD - 2, KD - 2, xt_lhs, banks)

        def act_mix_out(act, name, p):
            u0 = UNITS[name]
            for i in range(KD + 2):
                act_hi(act, u0 + i, None, BW).then_inc(hi_done, 1)
            act_result(act, p, 0)
            for i in range(KD + 2, 2 * KD):
                act_hi(act, u0 + i, None, BW).then_inc(hi_done, 1)

        def kv(odd):
            return (kTO, vO, KD) if odd else (kTE, vE, CL)

        def s_banks(s):
            return 2 + 3 * (s % 2)

        def pe_sample(pe, odd):
            kT, v, n = kv(odd)
            sa, sat = s_sa[odd], s_sat[odd]
            w = P // n

            def keys(s):
                g = NS * odd + s
                pe.wait_ge(kc_in[s % 2], 16 * ((NS // 2 + 2 * (s // 2 + 1)) if odd else s // 2 + 1))
                if g:
                    pe.wait_ge(kt_done, g)
                for c in range(n):
                    mm = nc.tensor.transpose(psf[:, c * P:(c + 1) * P], raw[:, s % 2, c * P:(c + 1) * P], ident)
                mm.then_inc(kt_mm, 1)

            def scores(s):
                g = NS * odd + s
                pe.wait_ge(kt_done, g + 1)
                pe.wait_ge(qb_done, g + 1)
                if s >= 2:
                    pe.wait_ge(sp_done, g - 1)
                b = s_banks(s)
                for m in range(1 + odd):
                    dst = bank(b + m, PAST + TS)
                    for i in range(CL):
                        c = CL * m + i
                        mm = nc.tensor.matmul(dst, qbd[:, c * P:(c + 1) * P], kts[s % 2][:, c, :],
                                              start=(i == 0), stop=(bool(odd) and i == CL - 1))
                    if not odd:
                        nc.tensor.matmul(dst, nlb, kts[s % 2][:, CL, :], start=False, stop=False)
                        nc.tensor.matmul(dst, lfp_b, kts[s % 2][:, CL + 1, :], start=False, stop=False)
                        mm = nc.tensor.matmul(dst, prod, ones3[:, 0:PAST + TS], start=False, stop=True)
                mm.then_inc(ssc_mm, 1)

            def turn(s):
                g = NS * odd + s
                pe.wait_ge(sa_done, g + 1)
                if g:
                    pe.wait_ge(sat_done, g)
                nc.tensor.transpose(bank(7, P), sa[:, 0:P], ident).then_inc(sat_mm, 1)
                if s == NS - 1:
                    nc.tensor.transpose(bank(6, P), sa[:, P:2 * P], ident).then_inc(pn_mm, 1)

            def output(s):
                g = NS * odd + s
                pe.wait_ge(sat_done, g + 1)
                pe.wait_ge(vc_in[s % 2], 16 * (NS // 2 * odd + s // 2 + 1))
                if g:
                    pe.wait_ge(so_done, g)
                for c in range(n):
                    mm = nc.tensor.matmul(bank(4, w, c * w), raw[:, 2 + s % 2, c * P:(c + 1) * P],
                                          sat[:, c * w:(c + 1) * w], start=True, stop=True)
                mm.then_inc(so_mm, 1)

            pe.wait_ge(t_out, 12 + 30 * odd)
            pe.wait_ge(tr_out, 10 + 20 * odd)
            if not odd:
                pe.wait_ge(cq_done, 1)
            keys(0)
            pe.wait_ge(t_out, 15 + 30 * odd)
            for s in range(NS + 1):
                if s < NS:
                    scores(s)
                if s:
                    turn(s - 1)
                if s + 1 < NS:
                    keys(s + 1)
                if s:
                    output(s - 1)
            pe.wait_ge(pn_done, odd + 1)
            wn = NH // n * P
            for c in range(n):
                mm = nc.tensor.matmul(psf[:, 2 * 512 + c * wn:2 * 512 + (c + 1) * wn], v[:, NP, c * P:(c + 1) * P],
                                      pn_flat[:, c * wn:(c + 1) * wn], start=True, stop=True)
            mm.then_inc(sn_mm, 1)
            pe.wait_ge(sn_done, odd + 1)
            for c in range(n):
                mm = nc.tensor.transpose(psf[:, 5 * 512 + c * P:5 * 512 + (c + 1) * P], view(scratch, c * P, P), ident)
            mm.then_inc(sot_mm, 1)

        def act_sample(act, odd):
            kT, v, n = kv(odd)
            sp_, sat = s_sp[odd], s_sat[odd]

            def keys(s):
                g = NS * odd + s
                act.wait_ge(kt_mm, g + 1)
                if s >= 2:
                    act.wait_ge(ssc_mm, g - 1)
                if s == 0:
                    act.wait_ge(rope_done if odd else ya_done, 2 if odd else CL)
                nc.scalar.activation(kts[s % 2][:, 0:n, 0:PAST], psf[:, 0:n * P].rearrange("p (c t) -> p c t", t=PAST),
                                     ACT.Copy).then_inc(kt_done, 1)

            def exps(s):
                g = NS * odd + s
                act.wait_ge(smax_done, g + 1)
                if g:
                    act.wait_ge(sa_done, g)
                for m in range(1 + odd):
                    e = nc.scalar.activation(sp_[:, m, :], bank(s_banks(s) + m, PAST + TS), ACT.Exp,
                                             bias=rneg[:, m, s % 2:s % 2 + 1], accum_out=rsum[:, m, s % 2:s % 2 + 1])
                e.then_inc(sp_done, 1)

            def turn(s):
                g = NS * odd + s
                act.wait_ge(sat_mm, g + 1)
                if g:
                    act.wait_ge(so_mm, g)
                nc.scalar.activation(sat, bank(7, P), ACT.Copy).then_inc(sat_done, 1)

            keys(0)
            for s in range(NS + 1):
                if s:
                    turn(s - 1)
                if s < NS:
                    exps(s)
                if s + 1 < NS:
                    keys(s + 1)
                if not odd and s < CL:
                    nc.scalar.activation(xT_hi[:, s, :], gate[:, s, :], ACT.Copy).then_inc(ya_hi, 1)

        def dve_sample_prepare(dve, odd):
            if not odd:
                dve.wait_ge(lf_in, 16)
                link(dve, nc.vector.tensor_scalar(nlb.rearrange("p (h q) -> p h q", q=TS),
                                                  lgf[:, NP, :].unsqueeze(2).to_broadcast([P, NH, TS]),
                                                  -1.0, None, ALU.mult))
                for i in range(2):
                    nc.vector.memset(kts[i][:, CL, :], 0.0)
                    nc.vector.memset(kts[i][:, CL + 1, PAST:], 0.0)
                    nc.vector.tensor_copy(kts[i][:, CL + 1, 0:PAST], con[:, C_SL:C_SL + PAST])
            link(dve, nc.vector.memset(qbd, 0.0) if odd else nc.vector.memset(qbd[:, 0:CL * P + P], 0.0))

        def dve_sample(dve, odd):
            kT, v, n = kv(odd)
            qT = qTO if odd else qTE
            sp_, sa = s_sp[odd], s_sa[odd]
            m = 1 + odd
            ot = view(scratch, 0, n, P)
            def fill(s):
                g, q0 = NS * odd + s, SEQ + TS * s
                if g:
                    dve.wait_ge(ssc_mm, g)
                if odd:
                    for c in range(4):
                        j, m = c % 2, c // 2
                        nc.vector.tensor_copy(
                            qbd[64 * j:64 * j + 64, BW * m:BW * m + CL * (P + 2 * TS)]
                            .rearrange("p (i x) -> p i x", i=CL)[:, :, TS * j:TS * (j + 1)],
                            qT[64 * j:64 * j + 64, CL * m:CL * (m + 1), q0:q0 + TS])
                else:
                    for j in range(2):
                        nc.vector.tensor_copy(
                            qbd[64 * j:64 * j + 64, TS * j:TS * j + CL * (P + 2 * TS)]
                            .rearrange("p (c x) -> p c x", x=P + 2 * TS)[:, :, 0:TS],
                            qT[64 * j:64 * j + 64, :, q0:q0 + TS])
                    nc.vector.tensor_tensor(prod.rearrange("p (h q) -> p h q", q=TS),
                                            lgf[:, NP, :].unsqueeze(2).to_broadcast([P, NH, TS]),
                                            con[:, C_UB + TS * s:C_UB + TS * (s + 1)].unsqueeze(1).to_broadcast([P, NH, TS]),
                                            ALU.mult)
                    nc.vector.tensor_copy(lfp_b.rearrange("p (h q) -> p h q", q=TS),
                                          lfp[:, s, :].unsqueeze(2).to_broadcast([P, NH, TS]))
                    nc.vector.tensor_copy(kts[s % 2][:, CL, PAST:], con[:, C_UB + TS * s:C_UB + TS * (s + 1)])
                nc.vector.tensor_copy(kts[s % 2][:, 0:n, PAST:PAST + TS], kT[:, :, q0:q0 + TS]).then_inc(qb_done, 1)

            def softmax(s):
                g, b, j = NS * odd + s, s_banks(s), s % 2
                dve.wait_ge(ssc_mm, g + 1)
                if not odd:
                    link(dve, nc.vector.tensor_tensor(bank(b, TS, PAST), bank(b, TS, PAST), con[:, C_NS:C_NS + TS], ALU.add))
                nc.vector.tensor_reduce(rneg[:, 0:m, j:j + 1], ps[:, b:b + m, 0:PAST + TS], AX.X, ALU.max,
                                        negate=True).then_inc(smax_done, 1)

            def normalize(s):
                g, j = NS * odd + s, s % 2
                dve.wait_ge(sp_done, g + 1)
                link(dve, nc.vector.reciprocal(rinv[:, 0:m, j:j + 1], rsum[:, 0:m, j:j + 1]))
                if g:
                    dve.wait_ge(sat_mm, g)
                mine = sa[:, P + TS * s:P + TS * (s + 1)]
                if odd:
                    link(dve, nc.vector.tensor_scalar(sp_[:, 1, :], sp_[:, 1, :], rinv[:, 1, j:j + 1], lamc[:, 1:2],
                                                      ALU.mult, ALU.mult))
                    nc.vector.scalar_tensor_tensor(sa[:, 0:P], sp_[:, 0, 0:P], rinv[:, 0, j:j + 1], sp_[:, 1, 0:P],
                                                   ALU.mult, ALU.add)
                    nc.vector.scalar_tensor_tensor(mine, sp_[:, 0, P:P + TS], rinv[:, 0, j:j + 1], sp_[:, 1, P:P + TS],
                                                   ALU.mult, ALU.add).then_inc(sa_done, 1)
                else:
                    nc.vector.tensor_scalar(sa[:, 0:P], sp_[:, 0, 0:P], rinv[:, 0, j:j + 1], None, ALU.mult)
                    nc.vector.tensor_scalar(mine, sp_[:, 0, P:P + TS], rinv[:, 0, j:j + 1], None,
                                            ALU.mult).then_inc(sa_done, 1)

            def out(s):
                dve.wait_ge(so_mm, NS * odd + s + 1)
                if odd:
                    nc.vector.tensor_copy(ot[:, :, TS * s:TS * (s + 1)],
                                          bank(4, P).rearrange("p (h q) -> p h q", q=TS)).then_inc(so_done, 1)
                else:
                    for j in range(2):
                        oc = nc.vector.tensor_copy(ot[64 * j:64 * j + 64, :, TS * s:TS * (s + 1)],
                                                   ps[64 * j:64 * j + 64, 4, 0:P]
                                                   .rearrange("p (c x) -> p c x", x=2 * TS)[:, :, TS * j:TS * (j + 1)])
                    oc.then_inc(so_done, 1)

            dve.wait_ge(tr_out, 10 + 20 * odd)
            fill(0)
            for s in range(NS):
                softmax(s)
                if s + 1 < NS:
                    fill(s + 1)
                if s:
                    out(s - 1)
                normalize(s)
                if not odd and s < CL:
                    dve.wait_ge(ya_hi, s + 1)
                    nc.vector.tensor_tensor(xT_lo[:, s, :], gate[:, s, :], xT_hi[:, s, :].bitcast(F32),
                                            ALU.subtract).then_inc(lru_end, 1)
            dve.wait_ge(pn_mm, odd + 1)
            mine = con[:, C_UB:C_UB + P].rearrange("p (s q) -> p s q", q=TS)[:, :, TS - 1]
            nc.vector.tensor_tensor(pn_b, bank(6, P).rearrange("p (h q) -> p h q", q=TS).unsqueeze(2).to_broadcast([P, NH, NS, TS]),
                                    mine.unsqueeze(1).unsqueeze(3).to_broadcast([P, NH, NS, TS]), ALU.mult).then_inc(pn_done, 1)
            out(NS - 1)
            dve.wait_ge(so_done, NS * (odd + 1))
            dve.wait_ge(sn_mm, odd + 1)
            if odd:
                nc.vector.tensor_tensor(ot, ot, psf[:, 2 * 512:2 * 512 + D].rearrange("p (h x) -> p h x", x=P),
                                        ALU.add).then_inc(sn_done, 1)
            else:
                for j in range(2):
                    rows = slice(64 * j, 64 * j + 64)
                    oc = nc.vector.tensor_tensor(ot[rows], ot[rows], psf[rows, 2 * 512:2 * 512 + D]
                                                 .rearrange("p (c e x) -> p c e x", c=CL, e=2)[:, :, j, :], ALU.add)
                oc.then_inc(sn_done, 1)
            dve.wait_ge(sot_mm, odd + 1)
            dve.wait_ge(k_out, 32 * (odd + 1))
            dve.wait_ge(v_out, 32 * (odd + 1))
            dst = tok[:, NP, :] if odd else tok[:, NP, LW:D]
            nc.vector.tensor_copy(dst, psf[:, 5 * 512:5 * 512 + n * P]).then_inc(sot_done, 1)

        def steps(odd):
            if odd:
                return [(i * NH + h, i, h) for i in range(NP) for h in range(NH)]
            return [(h * NP + i, i, h) for h in range(NH) for i in range(NP)]

        NSTEP = NP * NH
        BEHIND = (3, 2)

        def sc_bank(n, odd):
            return 2 * (n % 2) if odd else (0, 1, 7)[n % 3]

        def pe_prompt(pe, odd):
            st = steps(odd)
            g0 = NSTEP * odd
            d = BEHIND[odd]
            for j in range(NSTEP + d + 1):
                if j < NSTEP:
                    n, i, h = st[j]
                    g = g0 + n
                    w = (i + 1) * P
                    if n == 0:
                        pe.wait_ge(sot_done, odd + 1)
                        if not odd:
                            pe.wait_ge(hl_copied, 1)
                    if not odd:
                        if i == 0:
                            if h:
                                pe.wait_ge(nc_done, h)
                            for kb in range(NP):
                                for b in range(kb + 1):
                                    mm = nc.tensor.matmul(bank(6, P, kb * P), lgn[:, b, h:h + 1].to_broadcast([P, P]),
                                                          con[:, C_UT:C_UT + P] if b == kb else ones,
                                                          start=(b == 0), stop=(b == kb))
                            mm.then_inc(nc_mm, 1)
                        if n >= 3:
                            pe.wait_ge(s_read, g - 2)
                        c, pb = h // 2, 64 * (h % 2)
                        mm = nc.tensor.matmul(bank(sc_bank(n, odd), w), qTE[pb:pb + 64, c, i * P:(i + 1) * P],
                                              kTE[pb:pb + 64, c, 0:w], start=True, stop=True)
                    else:
                        if n >= 2:
                            pe.wait_ge(p_done, g - 1)
                        for m in range(2):
                            mm = nc.tensor.matmul(bank(sc_bank(n, odd) + m, w), qTO[64 * m:64 * m + 64, h, i * P:(i + 1) * P],
                                                  kTO[64 * m:64 * m + 64, h, 0:w], start=True, stop=True)
                    mm.then_inc(qk_mm, 1)
                if d <= j < NSTEP + d:
                    n, i, h = st[j - d]
                    g = g0 + n
                    pe.wait_ge(c_done if odd else p_done, g + 1)
                    if n >= 2:
                        pe.wait_ge(pt_done, g - 1)
                    b = (4 if odd else 2) + n % 2
                    src = pO[:, n % 3, 0, :] if odd else stE[:, n % 4, :]
                    for kb in range(i + 1):
                        mm = nc.tensor.transpose(bank(b, P, kb * P), src[:, kb * P:(kb + 1) * P], ident)
                    mm.then_inc(pt_mm, 1)
                if j > d:
                    n, i, h = st[j - d - 1]
                    g = g0 + n
                    pe.wait_ge(pt_done, g + 1)
                    if n >= 2:
                        pe.wait_ge(o_done, g - 1)
                    b = (6 if odd else 4) + n % 2
                    pt = (ptO if odd else ptE)[:, n % 2]
                    w = P if odd else DH
                    v = vO if odd else vE
                    for kb in range(i + 1):
                        mm = nc.tensor.matmul(bank(b, w), pt[:, kb, :], v[:, kb, h * w:(h + 1) * w],
                                              start=(kb == 0), stop=(kb == i))
                    mm.then_inc(pv_mm, 1)

        def act_prompt(act, odd):
            st = steps(odd)
            g0 = NSTEP * odd
            d = BEHIND[odd]
            for j in range(NSTEP + d):
                if j < NSTEP:
                    n, i, h = st[j]
                    g = g0 + n
                    w = (i + 1) * P
                    if not odd and i == 0:
                        act.wait_ge(nc_mm, h + 1)
                        if h >= 2:
                            act.wait_ge(s_read, NP * (h - 1))
                        elif h == 0:
                            act.wait_ge(sot_done, 1)
                        nc.scalar.activation(negc[:, h % 2, :], bank(6), ACT.Copy).then_inc(nc_done, 1)
                    act.wait_ge(s_ready, g + 1)
                    r = slice(n % 4, n % 4 + 1)
                    if odd:
                        if n >= 3:
                            act.wait_ge(pt_mm, g - 2)
                        elif n == 0:
                            act.wait_ge(sot_done, 2)
                        for m in range(2):
                            e = nc.scalar.activation(pO[:, n % 3, m, 0:w], bank(sc_bank(n, odd) + m, w), ACT.Exp,
                                                     bias=rneg[:, m, r], accum_out=rsum[:, m, r])
                    else:
                        e = nc.scalar.activation(stE[:, n % 4, 0:w], stE[:, n % 4, 0:w], ACT.Exp,
                                                 bias=rneg[:, 0, r], accum_out=rsum[:, 0, r])
                    e.then_inc(p_done, 1)
                if j >= d:
                    n, i, h = st[j - d]
                    g = g0 + n
                    act.wait_ge(pt_mm, g + 1)
                    if n >= 2:
                        act.wait_ge(pv_mm, g - 1)
                    w = (i + 1) * P
                    pt = (ptO if odd else ptE)[:, n % 2, 0:i + 1, :]
                    nc.scalar.activation(pt, bank((4 if odd else 2) + n % 2, w).rearrange("p (k n) -> p k n", n=P),
                                         ACT.Copy).then_inc(pt_done, 1)

        def dve_prompt(dve, odd):
            st = steps(odd)
            g0 = NSTEP * odd

            def scores(n, i, h):
                g, w = g0 + n, (i + 1) * P
                r = slice(n % 4, n % 4 + 1)
                dve.wait_ge(qk_mm, g + 1)
                if odd:
                    b = sc_bank(n, odd)
                    both = ps[0:CHUNK, b:b + 2, i * P + CHUNK:w]
                    link(dve, nc.vector.tensor_tensor(both, both, con[0:CHUNK, C_NC + CHUNK:C_NC + P].unsqueeze(1)
                                                      .to_broadcast([CHUNK, 2, P - CHUNK]), ALU.add))
                    nc.vector.tensor_reduce(rneg[:, :, r], ps[:, b:b + 2, 0:w], AX.X, ALU.max,
                                            negate=True).then_inc(s_ready, 1)
                    return
                if i == 0:
                    dve.wait_ge(nc_done, h + 1)
                if n >= 4:
                    dve.wait_ge(pt_mm, g - 3)
                s_t = stE[:, n % 4, :]
                nc.vector.scalar_tensor_tensor(s_t[:, 0:w], bank(sc_bank(n, odd), w), cq[:, i, h:h + 1],
                                               negc[:, h % 2, 0:w], ALU.add, ALU.add).then_inc(s_read, 1)
                dve.wait_ge(s_read, g + 1)
                link(dve, nc.vector.tensor_tensor(s_t[:, i * P:w], s_t[:, i * P:w], con[:, C_NT:C_NT + P], ALU.add))
                nc.vector.tensor_reduce(rneg[:, 0, r], s_t[:, 0:w], AX.X, ALU.max, negate=True).then_inc(s_ready, 1)

            def combine(n, i, h):
                g, w = g0 + n, (i + 1) * P
                r = slice(n % 4, n % 4 + 1)
                dve.wait_ge(p_done, g + 1)
                if not odd:
                    if n >= 4:
                        dve.wait_ge(o_done, g - 3)
                    nc.vector.reciprocal(rinv[:, 0, r], rsum[:, 0, r]).then_inc(c_done, 1)
                    return
                p1, p2 = pO[:, n % 3, 0, 0:w], pO[:, n % 3, 1, 0:w]
                link(dve, nc.vector.reciprocal(rinv[:, :, r], rsum[:, :, r]))
                link(dve, nc.vector.tensor_scalar(p2, p2, rinv[:, 1, r], lamc[:, 1:2], ALU.mult, ALU.mult))
                nc.vector.scalar_tensor_tensor(p1, p1, rinv[:, 0, r], p2, ALU.mult, ALU.add).then_inc(c_done, 1)

            def out(n, i, h):
                g = g0 + n
                dve.wait_ge(pv_mm, g + 1)
                if odd:
                    nc.vector.tensor_copy(tok[:, i, h * P:(h + 1) * P], bank(6 + n % 2, P)).then_inc(o_done, 1)
                else:
                    dve.wait_ge(c_done, g + 1)
                    nc.vector.tensor_scalar(tok[:, i, LW + h * DH:LW + (h + 1) * DH], bank(4 + n % 2, DH),
                                            rinv[:, 0, n % 4:n % 4 + 1], None, ALU.mult).then_inc(o_done, 1)

            if odd:
                dve.wait_ge(subg_in, 16)
                nc.vector.tensor_scalar(sub_g, sub_g, 1.0 - LAM_INIT, None, ALU.mult).then_inc(subg_done, 1)
                dve_subnorm(dve, NP)
            d = BEHIND[odd]
            for j in range(NSTEP + d + 1):
                if j < NSTEP:
                    scores(*st[j])
                if 1 <= j <= NSTEP:
                    combine(*st[j - 1])
                if j > d:
                    out(*st[j - d - 1])
                    if odd and (j - d) % NH == 0:
                        dve_subnorm(dve, (j - d) // NH - 1)

        def dve_subnorm(dve, t):
            if t < NP:
                dve.wait_ge(o_done, NSTEP + (t + 1) * NH)
            else:
                dve.wait_ge(sot_done, 2)
            k = (t + 1) % NT
            sq = scratch[:, :]
            link(dve, nc.vector.tensor_tensor(sq, tok[:, t, :], tok[:, t, :], ALU.mult))
            nc.vector.tensor_reduce(s_ss, sq.rearrange("p (h d) -> p h d", d=P), AX.X, ALU.add).then_inc(sq_done, 1)
            dve.wait_ge(srs_done, k + 1)
            heads = tok[:, t, :].rearrange("p (h d) -> p h d", d=P)
            nc.vector.tensor_tensor(heads, heads, s_rs.unsqueeze(2).to_broadcast([P, NH, P]), ALU.mult).then_inc(tok_ready, 1)

        def lru_u(c, j):
            return (u_pad[:, c, j:j + SEQ],
                    u_pad[:, c, UP:UW].rearrange("p (s x) -> p s x", x=US)[:, :, j:j + TS])

        def samples(t):
            return t[:, SEQ:TOK].rearrange("p (s x) -> p s x", x=TS)

        def dve_even_pairs(dve):
            u0, c0 = UNITS["EG"], CHUNKS["EG"]
            nc.vector.memset(u_pad[:, :, 0:CW - 1], 0.0)
            for c in range(CL):
                nc.vector.tensor_copy(u_pad[:, c, UP:UW].rearrange("p (s x) -> p s x", x=US)[:, :, 0:CW - 1],
                                      par[:, c, R_BUF:R_BUF + 24].rearrange("p (s x) -> p s x", x=CW - 1))
            for c in range(CL):
                n = D if c + 1 < CL else BW
                dve_lo(dve, u0 + 2 * c + 2, None, n).then_inc(lo_done, 1)
                for half in range(2):
                    at0, w = HALVES[half]
                    half_ready(dve, u0, c0, c, None, 0, half)
                    wp = min(at0 + w, SEQ) - at0
                    nc.vector.tensor_copy(u_pad[:, c, CW - 1 + at0:CW - 1 + at0 + wp], bank(4 * (c % 2) + half, wp))
                    if wp < w:
                        nc.vector.tensor_copy(lru_u(c, CW - 1)[1], bank(4 * (c % 2) + half, w - wp, wp)
                                              .rearrange("p (s x) -> p s x", x=TS))
                for half in range(2):
                    at0, w = HALVES[half]
                    half_ready(dve, u0, c0, c, None, 1, half)
                    nc.vector.tensor_copy(gate[:, c, at0:at0 + w], bank(4 * (c % 2) + 2 + half, w)).then_inc(h_done, 1)
                dve_lo(dve, u0 + 2 * c + 3, None, n).then_inc(lo_done, 1)
                dve.wait_ge(h_done, 2 * (c0 + c + 1))
                dve_conv(dve, c)
                if c == CL - 1:
                    dve_lo(dve, UNITS["ET"] + 2, None, BW).then_inc(lo_done, 1)
                dve_gelu(dve, c)

        def act_even_pairs(act):
            for c in range(CL):
                n = D if c + 1 < CL else BW
                for j in range(2):
                    act_hi(act, UNITS["EG"] + 2 * c + 2 + j, None, n).then_inc(hi_done, 1)
                if c:
                    act_gelu(act, c - 1)
            act_hi(act, UNITS["ET"] + 2, None, BW).then_inc(hi_done, 1)
            act_gelu(act, CL - 1)

        def pe_forget(pe):
            pe.wait_ge(wf_lo_done, 1)
            for half, (at0, w) in enumerate(HALVES):
                for k in range(KD):
                    for j, xt in enumerate((xT_lo, xT_hi)):
                        mm = nc.tensor.matmul(ps[0:2 * NH, 5 + half, 0:w], wf[:, k, :], xt[:, k, at0:at0 + w],
                                              start=(k == 0 and j == 0), stop=(k == KD - 1 and j == 1))
            mm.then_inc(f_mm, 1)

        def act_forget(act):
            act.wait_ge(f_mm, 1)
            for half, (at0, w) in enumerate(HALVES):
                nc.scalar.activation(f_rows[:, at0:at0 + w], ps[0:2 * NH, 5 + half, 0:w], ACT.Copy).then_inc(f_out, 1)

        def pe_forget_turn(pe):
            pe.wait_ge(f_out, 2)
            for t in range(NT):
                mm = nc.tensor.transpose(bank(7, 2 * NH, t * 2 * NH), f_rows[:, t * P:(t + 1) * P],
                                         con[0:2 * NH, C_ID:C_ID + 2 * NH])
            mm.then_inc(ft_mm, 1)

        def pe_cumulate(pe):
            pe.wait_ge(logf_done, 1)
            for i in range(NP):
                for b in range(i + 1):
                    mm = nc.tensor.matmul(bank(7, NH, 64 + i * NH), con[:, C_UT:C_UT + P] if b == i else ones,
                                          lgf[:, b, :], start=(b == 0), stop=(b == i))
            mm.then_inc(cq_mm, 1)

        def dve_forget(dve):
            dve.wait_ge(ft_mm, 1)
            logits = lsz[:, 0:NT * NH].rearrange("p (t h) -> p t h", h=NH)
            parts = bank(7, NT * 2 * NH).rearrange("p (t j h) -> p t j h", j=2, h=NH)
            link(dve, nc.vector.tensor_tensor(logits, parts[:, :, 1, :], bfb.unsqueeze(1).to_broadcast([P, NT, NH]), ALU.add))
            nc.vector.tensor_tensor(logits, logits, parts[:, :, 0, :], ALU.add)
            link(dve, nc.vector.tensor_copy(lsz[:, NT * NH:].unsqueeze(2), par[:, :, R_LAM:R_LAM + 1]))
            link(dve, nc.vector.tensor_scalar(lst1, lsz, -1.0, None, ALU.mult))
            nc.vector.tensor_tensor(lst1, lsz, lst1, ALU.max).then_inc(e_abs, 1)
            dve.wait_ge(e_exp, 1)
            link(dve, nc.vector.tensor_scalar(lst1, lst2, 2.0, None, ALU.add))
            link(dve, nc.vector.reciprocal(lst1, lst1))
            link(dve, nc.vector.tensor_tensor(lst1, lst2, lst1, ALU.mult))
            link(dve, nc.vector.tensor_tensor(lst3, lst1, lst1, ALU.mult))
            link(dve, nc.vector.tensor_scalar(lst2, lst3, 1.0 / 17, None, ALU.mult))
            for k in range(15, 1, -2):
                link(dve, nc.vector.scalar_tensor_tensor(lst2, lst2, 1.0 / k, lst3, ALU.add, ALU.mult))
            nc.vector.tensor_scalar(lst3, lsz, 0.0, None, ALU.min)
            link(dve, nc.vector.scalar_tensor_tensor(lst2, lst2, 1.0, lst1, ALU.add, ALU.mult))
            link(dve, nc.vector.scalar_tensor_tensor(ls_all, lst2, -2.0, lst3, ALU.mult, ALU.add))
            nc.vector.tensor_scalar(cl_a, ls_all[:, NT * NH:], 8.0, None, ALU.mult)
            nc.vector.tensor_scalar(cl_t, ls_all[:, NT * NH:], -8.0, None, ALU.mult)
            nc.vector.tensor_scalar(lgn, lgf, -1.0, None, ALU.mult).then_inc(logf_done, 1)

        LRU_AT = [(4, 5, 6), (7, 10, 11), (12, 13, 14), (15, 18, 19)]
        K_AT, Q_AT = 20, 22

        def dve_conv(dve, c):
            up, us = lru_u(c, 0)
            cp, cs = conv_u[:, c, 0:SEQ], samples(conv_u[:, c, :])
            w0, b0 = par[:, c, R_CW:R_CW + 1], par[:, c, R_CB:R_CB + 1]
            nc.vector.tensor_scalar(cp, up, w0, b0, ALU.mult, ALU.add)
            link(dve, nc.vector.tensor_scalar(cs, us, w0, b0, ALU.mult, ALU.add))
            for j in range(1, CW):
                up, us = lru_u(c, j)
                wj = par[:, c, R_CW + j:R_CW + j + 1]
                nc.vector.scalar_tensor_tensor(cp, up, wj, cp, ALU.mult, ALU.add)
                step = nc.vector.scalar_tensor_tensor(cs, us, wj, cs, ALU.mult, ALU.add)
                if j < CW - 1:
                    link(dve, step)
            step.then_inc(conv_done, 1)

        def dve_gelu(dve, c):
            g, z = gate[:, c, :], gelu_g[:, c, :]
            link(dve, nc.vector.tensor_tensor(z, g, g, ALU.mult))
            link(dve, nc.vector.tensor_scalar(z, z, 0.044715, 1.0, ALU.mult, ALU.add))
            nc.vector.tensor_tensor(z, z, g, ALU.mult).then_inc(gz_done, 1)

        def act_gelu(act, c):
            act.wait_ge(gz_done, c + 1)
            nc.scalar.activation(gelu_g[:, c, :], gelu_g[:, c, :], ACT.Sigmoid, scale=1.5957691216057308).then_inc(gs_done, 1)

        def pe_gates(pe, c):
            pe.wait_ge(conv_done, c + 1)
            if c == 0:
                pe.wait_ge(wg_in, 64)
                pe.wait_ge(e_abs, 1)
            else:
                pe.wait_ge(i_done, c)
            for j, cut in ((0, 512), (1, P)):
                lo_at, hi_at = ((5, 0), (6, 0)) if j == 0 else ((6, 512 - P), (7, 0))
                nc.tensor.matmul(bank(lo_at[0], cut, lo_at[1]), w_gate[:, c, j, :], conv_u[:, c, 0:cut], start=True, stop=True)
                mm = nc.tensor.matmul(bank(hi_at[0], TOK - cut, hi_at[1]), w_gate[:, c, j, :], conv_u[:, c, cut:TOK],
                                      start=True, stop=True)
            mm.then_inc(gate_mm, 1)

        def pe_between(pe, m):
            if m == 0:
                pe_forget(pe)
            if m == 1:
                pe_forget_turn(pe)
            for c in range(CL):
                if m == LRU_AT[c][0] - 2:
                    pe_gates(pe, c)
            if m == K_AT:
                pe.wait_ge(i_done, CL)
                pe_cumulate(pe)
                pe.wait_ge(t_out, 5)
                for t in range(NT):
                    pe_tr(pe, t, tok[:, t, LW:D])
            if m == Q_AT:
                pe.wait_ge(t_out, 10)
                for t in range(NT):
                    pe_tr(pe, NT + t, tok[:, t, 0:LW])

        def act_lru(act, c, step):
            if step == 0:
                act.wait_ge(gate_mm, c + 1)
                if c:
                    act.wait_ge(ya_done, c)
                nc.scalar.activation(r_c, psf[:, 5 * 512:5 * 512 + TOK], ACT.Sigmoid,
                                     bias=par[:, c, R_BR:R_BR + 1]).then_inc(r_done, 1)
                nc.scalar.activation(i_c, psf[:, 8 * 512 - TOK:8 * 512], ACT.Sigmoid,
                                     bias=par[:, c, R_BI:R_BI + 1]).then_inc(i_done, 1)
            elif step == 1:
                act.wait_ge(r_done, c + 1)
                if c == 0:
                    act.wait_ge(logf_done, 1)
                nc.scalar.activation(t_c, r_c, ACT.Tanh, scale=cl_t[:, c:c + 1]).then_inc(t_done, 1)
                act.wait_ge(t_done, c + 1)
                nc.scalar.activation(r_c, r_c, ACT.Exp, scale=cl_a[:, c:c + 1]).then_inc(a_done, 1)
            else:
                act.wait_ge(m2_done, c + 1)
                nc.scalar.activation(t_c, t_c, ACT.Sqrt).then_inc(m_done, 1)

        def act_even_blocks(act):
            act_forget(act)
            dests = [(lambda t: tok[:, t, LW:D], 1.0), (lambda t: tok[:, t, 0:LW], DH ** -0.5),
                     (lambda t: vE[:, t, :], 1.0)]
            for m in range(3, 3 * KD):
                act_hi(act, UNITS["ET"] + m, None, BW).then_inc(hi_done, 1)
                if m == 3:
                    act.wait_ge(e_abs, 1)
                    nc.scalar.activation(lst2, lst1, ACT.Exp, scale=-1.0).then_inc(e_exp, 1)
                if m % KD == 1 and m > KD:
                    b = m // KD - 1
                    act_block_out(act, "ET", b, dests[b][0], 0, dests[b][1])
                for c in range(CL):
                    for step in range(3):
                        if LRU_AT[c][step] == m:
                            act_lru(act, c, step)
            act_block_out(act, "ET", 2, dests[2][0], 0, dests[2][1])

        def dve_even_blocks(dve):
            link(dve, nc.vector.memset(hl, 0.0))
            for m in range(3, 3 * KD):
                dve_lo(dve, UNITS["ET"] + m, None, BW).then_inc(lo_done, 1)
                if m == 3:
                    dve_forget(dve)
                for c in range(CL):
                    for step in range(3):
                        if LRU_AT[c][step] == m:
                            dve_lru(dve, c, step)
                if m == K_AT + 2:
                    dve.wait_ge(cq_mm, 1)
                    nc.vector.tensor_copy(cq, bank(7, NP * NH, 64).rearrange("p (t h) -> p t h", h=NH)).then_inc(cq_done, 1)
                    dve.wait_ge(ya_done, CL)
                    for t in range(NT):
                        dve_tr(dve, t, tile_of(kTE, t))
                    dve_sample_prepare(dve, 0)
            for t in range(NT):
                dve_tr(dve, NT + t, tile_of(qTE, t))

        def dve_lru(dve, c, step):
            g_c = gelu_g[:, c, :]
            if step == 0:
                dve.wait_ge(i_done, c + 1)
                dve.wait_ge(conv_done, c + 1)
                link(dve, nc.vector.tensor_tensor(i_c, i_c, conv_u[:, c, :], ALU.mult))
                dve.wait_ge(gs_done, c + 1)
                link(dve, nc.vector.tensor_tensor(g_c, g_c, gate[:, c, :], ALU.mult))
            elif step == 1:
                dve.wait_ge(t_done, c + 1)
                d_c = conv_u[:, c, :]
                link(dve, nc.vector.tensor_scalar(d_c, t_c, 1.0, None, ALU.add))
                link(dve, nc.vector.reciprocal(d_c, d_c))
                nc.vector.scalar_tensor_tensor(t_c, t_c, 2.0, d_c, ALU.mult, ALU.mult).then_inc(m2_done, 1)
                dve.wait_ge(a_done, c + 1)
                first_a = samples(r_c)[:, :, 0:1]
                link(dve, nc.vector.tensor_tensor(h0a.unsqueeze(2), first_a, par[:, c, R_H0:R_H0 + NS].unsqueeze(2), ALU.mult))
                link(dve, nc.vector.memset(first_a, 0.0))
                nc.vector.tensor_copy(hl[:, c, 9:12], u_pad[:, c, SEQ:UP])
                nc.vector.tensor_copy(hl[:, c, 12:36].rearrange("p (s x) -> p s x", x=CW - 1),
                                      u_pad[:, c, UP:UW].rearrange("p (s x) -> p s x", x=US)[:, :, TS:US])
            else:
                dve.wait_ge(m_done, c + 1)
                first_b = samples(i_c)[:, :, 0:1]
                link(dve, nc.vector.tensor_tensor(i_c, i_c, t_c, ALU.mult))
                link(dve, nc.vector.tensor_tensor(first_b, first_b, h0a.unsqueeze(2), ALU.add))
                link(dve, nc.vector.tensor_tensor_scan(t_c, r_c, i_c, 0.0, ALU.mult, ALU.add))
                nc.vector.tensor_copy(hl[:, c, 0:1], t_c[:, SEQ - 1:SEQ])
                nc.vector.tensor_copy(hl[:, c, 1:9].unsqueeze(2), samples(t_c)[:, :, TS - 1:TS]).then_inc(hl_ready, 1)
                nc.vector.tensor_tensor(gate[:, c, :], t_c, g_c, ALU.mult).then_inc(ya_done, 1)

        def pe_last_rows(pe):
            pe.wait_ge(hl_ready, CL)
            for c in range(CL):
                mm = nc.tensor.transpose(bank(7, P, c * P), hl[:, c, :], ident)
            mm.then_inc(hl_ps, 1)

        def rope(dve, k):
            xs = tok[:, :, :].rearrange("p t (s e) -> p t s e", e=DH)
            x1, x2 = xs[:, :, :, 0:8], xs[:, :, :, 8:16]
            cb = cosb.unsqueeze(2).to_broadcast([P, NT, 2 * NH, 8])
            sn = sinb.unsqueeze(2).to_broadcast([P, NT, 2 * NH, 8])
            nc.vector.tensor_tensor(rot[0], x1, cb, ALU.mult)
            nc.vector.tensor_tensor(rot[1], x2, sn, ALU.mult)
            nc.vector.tensor_tensor(rot[2], x2, cb, ALU.mult)
            link(dve, nc.vector.tensor_tensor(rot[3], x1, sn, ALU.mult))
            nc.vector.tensor_tensor(x1, rot[0], rot[1], ALU.subtract)
            nc.vector.tensor_tensor(x2, rot[2], rot[3], ALU.add).then_inc(rope_done, 1)

        def tile_of(t, n):
            return t[:, :, n * P:(n + 1) * P]

        A, E, O = (lambda f: (UNITS["A%d" % f], D)), (UNITS["EG"], D), (UNITS["OT"], BW)

        @block.scalar
        def _(act):
            act.dma_start(con[:, :], a["consts"]).then_inc(con_in, 16)
            act_norm(act, -1, A(0))
            act.wait_ge(par_in, 16 * 9)
            act.wait_ge(lam_sum, 1)
            nc.scalar.activation(lamc[:, 2:4], lamc[:, 0:2], ACT.Exp).then_inc(lam_exp, 1)
            nc.scalar.activation(wf[:, :, 0:NH], wf_raw, ACT.Copy).then_inc(wf_hi_done, 1)
            act_ffn(act, 0, 0)
            act_norm(act, 0, E)
            act_even_pairs(act)
            act_even_blocks(act)
            act_sample(act, 0)
            act.wait_ge(hl_ps, 1)
            nc.scalar.activation(hl_rows[0:64, :], ps[0:64, 7, :], ACT.Copy).then_inc(hl_copied, 1)
            act_prompt(act, 0)
            for t in range(NT):
                act_xt(act, "yE", t, t, CL)
            act_mix_out(act, "EO", 1)
            act_norm(act, 1, A(1))
            act_ffn(act, 1, 2)
            act_norm(act, 2, A(2))
            act_ffn(act, 2, 3)
            act_norm(act, 3, O)

            def before(b):
                if b == 3:
                    act.wait_ge(tr_mm, 20)
                    act.wait_ge(k_out, 64)
            act_blocks(act, "OT", [lambda t: tok[:, t, 0:BW], lambda t: tok[:, t, BW:D],
                                   lambda t: vO[:, t, 0:BW], lambda t: tok[:, t, 0:BW],
                                   lambda t: tok[:, t, BW:D], lambda t: vO[:, t, BW:D]],
                       15, [1.0] * 3 + [DH ** -0.5] * 2 + [1.0], before)
            act_sample(act, 1)
            act_prompt(act, 1)
            for j in range(NT):
                act_xt(act, "yO", j, (j + NP) % NT)
            act_mix_out(act, "OO", 4)
            act_norm(act, 4, A(3))
            act_ffn(act, 3, 5)
            act_norm(act, 5)

        @block.vector
        def _(dve):
            for t in range(NT):
                dve.wait_ge(x_in[t], 16)
            dve_norm(dve, -1, A(0))
            dve.wait_ge(par_in, 16 * 9)
            link(dve, nc.vector.tensor_tensor(lam_pr, lam_in[:, 0:4:2, :], lam_in[:, 1:4:2, :], ALU.mult))
            nc.vector.tensor_reduce(lamc[:, 0:2], lam_pr, AX.X, ALU.add).then_inc(lam_sum, 1)
            dve.wait_ge(lam_exp, 1)
            link(dve, nc.vector.tensor_tensor(lamc[:, 0:1], lamc[:, 2:3], lamc[:, 3:4], ALU.subtract))
            link(dve, nc.vector.tensor_scalar(lamc[:, 0:1], lamc[:, 0:1], LAM_INIT, None, ALU.add))
            nc.vector.tensor_scalar(lamc[:, 1:2], lamc[:, 0:1], -1.0, None, ALU.mult)
            dve.wait_ge(wf_hi_done, 1)
            nc.vector.tensor_tensor(wf[:, :, NH:], wf_raw, wf[:, :, 0:NH].bitcast(F32), ALU.subtract).then_inc(wf_lo_done, 1)
            dve.wait_ge(par_ps, 1)
            nc.vector.tensor_copy(par[:, :, :], bank(7, CL * R_ALL).rearrange("p (c r) -> p c r", r=R_ALL)).then_inc(par_done, 1)
            dve_ffn(dve, 0)
            dve_norm(dve, 0, E)
            dve_even_pairs(dve)
            dve_even_blocks(dve)
            dve_sample(dve, 0)
            dve_prompt(dve, 0)
            for t in range(NT):
                dve_xt(dve, "yE", t, t, CL)
            dve_units(dve, UNITS["EO"], 2 * KD)
            dve_norm(dve, 1, A(1))
            dve_ffn(dve, 1)
            dve_norm(dve, 2, A(2))
            dve_ffn(dve, 2)
            dve_norm(dve, 3, O)
            u = UNITS["OT"]
            dve_units(dve, u + 2, 2 * KD)
            dve.wait_ge(t_out, 15 + 10)
            rope(dve, 0)
            dve_pairs(dve, 0)
            dve_units(dve, u + 2 + 2 * KD, KD)
            for t in range(NT):
                for j in range(2):
                    dve_tr(dve, 10 + 2 * t + j, tile_of(kTO, t)[:, 4 * j:4 * j + 4, :])
            dve_units(dve, u + 2 + 3 * KD, 2 * KD)
            dve.wait_ge(t_out, 15 + 25)
            rope(dve, 1)
            dve_pairs(dve, 1)
            dve_units(dve, u + 2 + 5 * KD, KD - 2)
            dve_sample_prepare(dve, 1)
            for t in range(NT):
                for j in range(2):
                    dve_tr(dve, 20 + 2 * t + j, tile_of(qTO, t)[:, 4 * j:4 * j + 4, :])
            dve_sample(dve, 1)
            dve_prompt(dve, 1)
            for j in range(NT):
                dve_xt(dve, "yO", j, (j + NP) % NT)
            dve_units(dve, UNITS["OO"], 2 * KD)
            dve_norm(dve, 4, A(3))
            dve_ffn(dve, 3)
            dve_norm(dve, 5)

        @block.tensor
        def _(pe):
            pe.wait_ge(con_in, 16)

            def parameters():
                pe.wait_ge(par_in, 16 * 9)
                for c in range(CL):
                    mm = nc.tensor.transpose(bank(7, R_ALL, c * R_ALL), prow[0:R_ALL, c * P:(c + 1) * P],
                                             con[0:R_ALL, C_ID:C_ID + R_ALL])
                mm.then_inc(par_ps, 1)

            pe_pairs(pe, "A0", 0, KF, parameters)
            pe_ffn_out(pe, 0, 0)
            pe_pairs(pe, "EG", 1, CL)
            pe_blocks(pe, "ET", 0, 3, 0,
                      lambda t: pe.wait_ge(h_done, 2 * (CHUNKS["EG"] + CL) - (0 if t == 4 else 2)),
                      lambda m: pe_between(pe, m))
            pe_sample(pe, 0)
            pe_last_rows(pe)
            pe_prompt(pe, 0)
            pe.wait_ge(o_done, NSTEP)
            for t in range(NT):
                pe_xt(pe, "yE", t, t, CL)
            pe_mix_out(pe, "EO", 1, "yE")
            pe_pairs(pe, "A1", 2, KF)
            pe_ffn_out(pe, 1, 2)
            pe_pairs(pe, "A2", 3, KF)
            pe_ffn_out(pe, 2, 3)
            pe_norm(pe, 4)
            pe_blocks(pe, "OT", 0, 3, 15, lambda t: pe.wait_ge(xt_lo, XT["pre4"] + NT))
            pe.wait_ge(rope_done, 1)
            pe_tr_odd(pe, 10)
            pe_blocks(pe, "OT", 3, 3, 30)
            pe.wait_ge(rope_done, 2)
            pe_tr_odd(pe, 20)
            pe_sample(pe, 1)
            pe_prompt(pe, 1)
            for j in range(NT):
                if j == 1:
                    pe.wait_ge(o_done, 2 * NSTEP)
                pe_xt(pe, "yO", j, (j + NP) % NT)
            pe_mix_out(pe, "OO", 4, "yO")
            pe_pairs(pe, "A3", 5, KF)
            pe_ffn_out(pe, 3, 5)

        @block.gpsimd
        def _(pool):
            pool_gain_pre(pool, 0)
            nc.gpsimd.memset(nhalf, -0.5).then_inc(gs, 1)
            pool_count[0] += 1
            pool.wait_ge(gs, pool_count[0])
            rows = [(R_BUF, 24, a["state_lru_conv"][0].rearrange("s j c -> (s j) c")),
                    (R_H0, NS, a["state_lru_h"][0]), (R_CW, CW, a["lru_conv_w"][0]),
                    (R_CB, 1, a["lru_conv_b"]), (R_LAM, 1, a["lru_lambda"])]
            for r, n, src in rows:
                pool.dma_start(prow[r:r + n, :], src).then_inc(par_in, 16)
            pool.dma_start(prow[R_BR:R_BI + 1, :].rearrange("j (n g) -> j n g", g=DH),
                           a["lru_b_gates"][0].rearrange("n (j g) -> j n g", g=DH)).then_inc(par_in, 16)
            pool.dma_start(wf_raw, a["w_in_even"][0].rearrange("(k p) n -> p k n", p=P)[:, :, 2 * LW + 3 * LW:])\
                .then_inc(par_in, 16)
            pool.dma_start(bfb, a["b_fox_f"][0].partition_broadcast(P)).then_inc(par_in, 16)
            pool.dma_start(lam_in.rearrange("p a b -> p (a b)"), a["diff_lambda"][0].rearrange("a b -> (a b)")
                           .partition_broadcast(P)).then_inc(par_in, 16)
            pool_gain_post(pool, 0)
            pool_norm(pool, -1)
            pool_gain_pre(pool, 1)
            pool_norm(pool, 0)
            pool_gain_post(pool, 1)
            pool_gain_pre(pool, 2)
            pool.wait_ge(lo_done, UNITS["EG"])
            nc.gpsimd.memset(w_gate, 0.0).then_inc(gs, 1)
            pool_count[0] += 1
            pool.wait_ge(gs, pool_count[0])
            for e in range(2):
                for j in range(2):
                    pool.dma_start(w_gate[64 * e:64 * e + 64, :, j, 64 * e:64 * e + 64],
                                   a["lru_w_gates"][0, e:8:2, :, 64 * j:64 * j + 64].rearrange("c k g -> k c g"))\
                        .then_inc(wg_in, 16)
            pool.dma_start(lfp, a["cache_fox_logf"][0].rearrange("s t h -> t s h")).then_inc(lf_in, 16)

            def store(name, tile, done):
                pool.dma_start(o["p_" + name][0, 0].rearrange("(t p) h d -> p t (h d)", p=P), tile[:, 0:NP, :])\
                    .then_inc(done, 16)
                pool.dma_start(o["s_" + name][0].rearrange("s t h d -> (s t) (h d)"), tile[:, NP, :]).then_inc(done, 16)

            pool.wait_ge(t_out, 5)
            store("fox_k", tok[:, :, LW:D], k_out)
            pool.wait_ge(t_out, 15)
            store("fox_v", vE, v_out)
            pool.wait_ge(logf_done, 1)
            pool.dma_start(o["p_fox_logf"][0, 0].rearrange("(t p) h -> p t h", p=P), lgf[:, 0:NP, :]).then_inc(out_sem2, 16)
            pool.dma_start(o["s_fox_logf"][0].rearrange("s t h -> (s t) h"), lgf[:, NP, :]).then_inc(out_sem2, 16)
            pool.wait_ge(hl_copied, 1)
            for name, r, n, form in [("p_lru_h", 0, 1, None), ("s_lru_h", 1, NS, None),
                                     ("p_lru_conv", 9, 3, "s j c -> (s j) c"), ("s_lru_conv", 12, 24, "s j c -> (s j) c")]:
                dst = o[name][0]
                pool.dma_start(dst.rearrange(form) if form else dst, hl_rows[r:r + n, :]).then_inc(out_sem2, 16)
            pool.wait_ge(out_sem2, 16 * 6)
            pool_norm(pool, 1)
            pool_gain_post(pool, 2)
            pool_gain_pre(pool, 3)
            pool_norm(pool, 2)
            pool_gain_post(pool, 3)
            pool_gain_pre(pool, 4)
            pool_norm(pool, 3)
            pool.dma_start(sub_g, a["diff_subln_g"][0].unsqueeze(1)).then_inc(subg_in, 16)
            pool.wait_ge(rope_done, 1)
            store("diff_k", tok, k_out)
            pool.wait_ge(t_out, 15 + 30)
            store("diff_v", vO, v_out)
            for k in range(NT):
                pool.wait_ge(sq_done, k + 1)
                nc.gpsimd.tensor_scalar(s_ss, s_ss, 1.0 / P, EPS, ALU.mult, ALU.add).then_inc(gs, 1)
                pool_count[0] += 1
                pool.wait_ge(gs, pool_count[0])
                nc.gpsimd.tensor_tensor(s_rs, s_ss, nhalf.to_broadcast([P, NH]), ALU.pow).then_inc(srs_done, 1)
            pool_gain_post(pool, 4)
            pool_gain_pre(pool, 5)
            pool_norm(pool, 4)
            pool_gain_post(pool, 5)
            pool_norm(pool, 5)


_INS = ['x_prompt', 'x_sample', 'cache_fox_k', 'cache_fox_v', 'cache_fox_logf', 'state_lru_h', 'state_lru_conv',
        'cache_diff_k', 'cache_diff_v', 'norm_g', 'w_ffn_in', 'w_ffn_out', 'w_in_even', 'b_fox_f', 'lru_conv_w',
        'lru_conv_b', 'lru_w_gates', 'lru_b_gates', 'lru_lambda', 'w_out_even', 'w_in_odd', 'diff_lambda',
        'diff_subln_g', 'w_out_odd']


def _group(prefix, b, t):
    return [(prefix + 'fox_k', (1, b, t, NH, DH)), (prefix + 'fox_v', (1, b, t, NH, DH)),
            (prefix + 'fox_logf', (1, b, t, NH)), (prefix + 'lru_h', (1, b, LW)),
            (prefix + 'lru_conv', (1, b, CW - 1, LW)), (prefix + 'diff_k', (1, b, t, NH, P)),
            (prefix + 'diff_v', (1, b, t, NH, P))]


_OUTS = [('y_prompt', (1, SEQ, D)), ('y_sample', (NS, TS, D))] + _group('p_', 1, SEQ) + _group('s_', NS, TS)


def _constants():
    import numpy as np
    i, j = np.arange(P)[:, None], np.arange(P)[None, :]
    c = np.zeros((P, C_ALL), np.float32)
    c[:, C_ID:C_ID + P] = i == j
    c[:, C_UT:C_UT + P] = i <= j
    c[:, C_ONE:C_ONE + 3 * P] = 1
    c[:, C_SL:C_SL + P] = i > j
    c[:, C_NT:C_NT + P] = np.where(j > i, NEG, 0)
    c[:, C_NC:C_NC + P] = np.where(j // CHUNK > i // CHUNK, NEG, 0)
    c[:, C_UB:C_UB + P] = (i // TS == j // TS) & (i <= j)
    pos = np.concatenate([np.arange(SEQ), PAST + np.tile(np.arange(TS), NS)]).astype(np.float32).reshape(NT, P).T
    inv = (np.float32(500000.0) ** (-np.arange(8, dtype=np.float32) * np.float32(2.0 / 16))).astype(np.float32)
    ang = (pos[:, :, None] * inv).astype(np.float32)
    c[:, C_COS:C_COS + NT * 8] = np.cos(ang).reshape(P, -1)
    c[:, C_SIN:C_SIN + NT * 8] = np.sin(ang).reshape(P, -1)
    c[:, C_NS:C_NS + TS] = np.where(np.arange(TS)[None, :] > i % TS, NEG, 0)
    return c


def kernel(**inputs):
    import numpy as _np
    import concourse.bacc as _bacc
    from concourse.bass_utils import run_bass_kernel_spmd as _run

    nc = _bacc.Bacc("TRN2", target_bir_lowering=False, num_devices=1)
    arrays, ins, outs = {}, {}, {}
    for name, v in [(n, inputs[n]) for n in _INS] + [("consts", _constants())]:
        v = _np.ascontiguousarray(v)
        arrays["in_" + name] = v
        ins[name] = nc.dram_tensor("in_" + name, v.shape, F32, kind="ExternalInput").ap()
    for name, shape in _OUTS:
        outs[name] = nc.dram_tensor("out_" + name, shape, F32, kind="ExternalOutput").ap()
    build_trunk(nc, ins, outs)
    r = _run(nc, [arrays], core_ids=[0])
    return tuple(r.results[0]["out_" + name] for name, _ in _OUTS)
```
